# Optimizing a Trainium2 kernel written in Bass

```python
import math
import jax, jax.numpy as jnp
from jax import lax
import numpy as np

'''One inference step of a 4-layer hybrid decoder trunk (interleaved RWKV-7 / HGRN2).

Layer i uses token mixer (i mod 2): even layers = RWKV-7 time mixing, odd layers = HGRN2.
Each layer: x <- x + RMSNorm_post( Mixer( RMSNorm_pre(x) ) ); each mixer branch carries a
full-width SiLU gate path (Mamba-style widening) that multiplies the branch output before
its output projection; there is no separate channel mixer.

Inputs:
  x_prompt          (BATCH, SEQ, D_MODEL)        new sequences, positions 0..SEQ-1
  x_sample          (DEC_BATCH, DEC_SEQ, D_MODEL) new tokens at positions PAST_LEN..PAST_LEN+DEC_SEQ-1
  state_rwkv_shift  (N_RWKV, DEC_BATCH, D_MODEL) last pre-normed row seen by each RWKV layer (token shift)
  state_rwkv_wkv    (N_RWKV, DEC_BATCH, RWKV_HEADS, RWKV_HEAD, RWKV_HEAD) RWKV-7 matrix state [value, key]
  state_hgrn        (N_HGRN, DEC_BATCH, HGRN_HEADS, HGRN_DK, HGRN_DV) HGRN2 expanded state
  + weights.
Returns the tuple
  (y_prompt (BATCH, SEQ, D_MODEL), y_sample (DEC_BATCH, DEC_SEQ, D_MODEL),
   prompt_rwkv_shift (N_RWKV, BATCH, D_MODEL), prompt_rwkv_wkv (N_RWKV, BATCH, RWKV_HEADS, RWKV_HEAD, RWKV_HEAD),
   prompt_hgrn (N_HGRN, BATCH, HGRN_HEADS, HGRN_DK, HGRN_DV),
   sample_rwkv_shift (N_RWKV, DEC_BATCH, D_MODEL), sample_rwkv_wkv (N_RWKV, DEC_BATCH, RWKV_HEADS, RWKV_HEAD, RWKV_HEAD),
   sample_hgrn (N_HGRN, DEC_BATCH, HGRN_HEADS, HGRN_DK, HGRN_DV))
'''

D_MODEL = 2048
BATCH = 1
SEQ = 512
DEPTH = 2
DEC_BATCH = 8
DEC_SEQ = 4
PAST_LEN = 4096
PAGE_SIZE = 128

N_MIXERS = 2
N_RWKV = (DEPTH + 1) // 2
N_HGRN = DEPTH // 2
RWKV_HEAD = 64
RWKV_HEADS = D_MODEL // RWKV_HEAD
RWKV_DECAY_LORA = max(32, int(round(1.8 * D_MODEL ** 0.5 / 32)) * 32)
RWKV_AAA_LORA = max(32, int(round(1.8 * D_MODEL ** 0.5 / 32)) * 32)
RWKV_MV_LORA = max(32, int(round(1.3 * D_MODEL ** 0.5 / 32)) * 32)
RWKV_GN_EPS = 1e-5 * RWKV_HEAD
N_SHIFT_MIX = 6
HGRN_EXPAND = 128
HGRN_HEADS = D_MODEL // HGRN_EXPAND
HGRN_DK = HGRN_EXPAND
HGRN_DV = D_MODEL // HGRN_HEADS
HGRN_CHUNK = 64
NORM_EPS = 1e-6
GATE_FLOOR = 1e-30

kernel_name = 'hybrid_rwkv7_hgrn2_decode_step'

def rms_norm(x, w):
    x32 = x.astype(jnp.float32)
    y = x32 * lax.rsqrt(jnp.mean(x32 * x32, axis=-1, keepdims=True) + NORM_EPS)
    return (y * w.astype(jnp.float32)).astype(x.dtype)

def rwkv7_mix(x, shift_prev, wkv_prev, v_first, vres, mu, w_in, w0, w1, w2, a0, a1, a2,
              k_k, k_a, r_k, ln_w, ln_b, w_o):
    B, T, D = x.shape
    f32 = jnp.float32
    x_prev = jnp.concatenate([shift_prev[:, None, :].astype(x.dtype), x[:, :-1]], axis=1)
    xs = x[:, :, None, :] + (x_prev - x)[:, :, None, :] * mu
    proj = jnp.einsum('btnd,nde->btne', xs[:, :, :4], w_in)
    r, k, v, z = proj[:, :, 0], proj[:, :, 1], proj[:, :, 2], proj[:, :, 3]
    xv, xw, xa = xs[:, :, 2], xs[:, :, 4], xs[:, :, 5]
    w_log = -jax.nn.softplus(-(w0 + jnp.tanh(xw @ w1) @ w2)) - 0.5
    decay = jnp.exp(-jnp.exp(w_log.astype(f32)))
    if vres is None:
        v_first = v
    else:
        v0, v1, v2 = vres
        v = v + (v_first - v) * jax.nn.sigmoid(v0 + (xv @ v1) @ v2)
    a = jax.nn.sigmoid(a0 + (xa @ a1) @ a2)
    heads = lambda t: t.reshape(B, T, RWKV_HEADS, RWKV_HEAD).astype(f32)
    kk = heads(k * k_k)
    kk = kk / jnp.maximum(jnp.sqrt(jnp.sum(kk * kk, axis=-1, keepdims=True)), 1e-12)
    k = k * (1.0 + (a - 1.0) * k_a)
    rh, kh, vh, ah, wh = heads(r), heads(k), heads(v), heads(a), heads(decay)
    bh = kk * ah

    def step(S, inp):
        r_t, w_t, k_t, v_t, kk_t, b_t = inp
        sa = jnp.einsum('bhvk,bhk->bhv', S, -kk_t)
        S = S * w_t[:, :, None, :] + sa[..., None] * b_t[:, :, None, :] + v_t[..., None] * k_t[:, :, None, :]
        return S, jnp.einsum('bhvk,bhk->bhv', S, r_t)

    tm = lambda t: jnp.moveaxis(t, 1, 0)
    S_fin, y = lax.scan(step, wkv_prev.astype(f32), (tm(rh), tm(wh), tm(kh), tm(vh), tm(kk), tm(bh)))
    y = jnp.moveaxis(y, 0, 1)
    mean = jnp.mean(y, axis=-1, keepdims=True)
    var = jnp.mean(jnp.square(y - mean), axis=-1, keepdims=True)
    y = ((y - mean) * lax.rsqrt(var + RWKV_GN_EPS)).reshape(B, T, D) * ln_w + ln_b
    bonus = jnp.sum(rh * kh * r_k, axis=-1, keepdims=True) * vh
    y = y + bonus.reshape(B, T, D)
    out = (y.astype(x.dtype) * jax.nn.silu(z)) @ w_o
    return out, x[:, -1], S_fin, v_first

def hgrn2_mix(x, S_prev, lb, w_in, norm_w, w_o):
    B, T, D = x.shape
    f32 = jnp.float32
    q, f_logit, i, z = jnp.split(x @ w_in, 4, axis=-1)
    f_logit = f_logit.astype(f32)
    f = lb + (1.0 - lb) * jax.nn.sigmoid(f_logit)
    log_f = jnp.log(jnp.maximum(f, GATE_FLOOR))
    k = (1.0 - lb) * jax.nn.sigmoid(-f_logit)
    q = jax.nn.silu(q.astype(f32)) * HGRN_DK ** -0.5
    c = math.gcd(T, HGRN_CHUNK)
    nc = T // c
    chunks = lambda t, d: t.reshape(B, nc, c, HGRN_HEADS, d).transpose(1, 0, 3, 2, 4)
    qc, kc = chunks(q, HGRN_DK), chunks(k, HGRN_DK)
    vc = chunks(i.astype(f32), HGRN_DV)
    gc = jnp.cumsum(chunks(log_f, HGRN_DK), axis=3)
    mask = jnp.tril(jnp.ones((c, c), dtype=bool))[:, :, None]

    def chunk_step(S, inp):
        q_c, k_c, v_c, G = inp
        diff = G[:, :, :, None, :] - G[:, :, None, :, :]
        dec = jnp.where(mask, jnp.exp(jnp.minimum(diff, 0.0)), 0.0)
        A = jnp.einsum('bhtd,bhsd,bhtsd->bhts', q_c, k_c, dec)
        o = jnp.einsum('bhts,bhse->bhte', A, v_c) + jnp.einsum('bhtd,bhde->bhte', q_c * jnp.exp(G), S)
        G_last = G[:, :, -1:, :]
        S = jnp.exp(G_last[:, :, 0, :, None]) * S + jnp.einsum('bhsd,bhse->bhde', k_c * jnp.exp(G_last - G), v_c)
        return S, o

    S_fin, o = lax.scan(chunk_step, S_prev.astype(f32), (qc, kc, vc, gc))
    o = o.transpose(1, 0, 3, 2, 4).reshape(B, T, HGRN_HEADS, HGRN_DV)
    o = o * lax.rsqrt(jnp.mean(o * o, axis=-1, keepdims=True) + NORM_EPS) * norm_w
    out = (o.reshape(B, T, D).astype(x.dtype) * jax.nn.silu(z)) @ w_o
    return out, S_fin

def setup_inputs(seed: int = 0) -> dict:
    key = jax.random.key(seed)
    ks = jax.random.split(key, 32)
    f32 = jnp.float32
    D = D_MODEL
    nrm = lambda kk, shape, s: s * jax.random.normal(kk, shape, f32)
    return {
        'x_prompt': nrm(ks[0], (BATCH, SEQ, D), 1.0),
        'x_sample': nrm(ks[1], (DEC_BATCH, DEC_SEQ, D), 1.0),
        'state_rwkv_shift': nrm(ks[2], (N_RWKV, DEC_BATCH, D), 1.0),
        'state_rwkv_wkv': nrm(ks[3], (N_RWKV, DEC_BATCH, RWKV_HEADS, RWKV_HEAD, RWKV_HEAD), 0.5),
        'state_hgrn': nrm(ks[4], (N_HGRN, DEC_BATCH, HGRN_HEADS, HGRN_DK, HGRN_DV), 0.5),
        'norm_pre': 1.0 + nrm(ks[5], (DEPTH, D), 0.02),
        'norm_post': 1.0 + nrm(ks[6], (DEPTH, D), 0.02),
        'rwkv_mu': jax.random.uniform(ks[7], (N_RWKV, N_SHIFT_MIX, D), f32),
        'rwkv_w_in': nrm(ks[8], (N_RWKV, 4, D, D), D ** -0.5),
        'rwkv_w0': jax.random.uniform(ks[9], (N_RWKV, D), f32, -4.0, 1.0),
        'rwkv_w1': nrm(ks[10], (N_RWKV, D, RWKV_DECAY_LORA), D ** -0.5),
        'rwkv_w2': nrm(ks[11], (N_RWKV, RWKV_DECAY_LORA, D), 0.1 * RWKV_DECAY_LORA ** -0.5),
        'rwkv_a0': nrm(ks[12], (N_RWKV, D), 0.1),
        'rwkv_a1': nrm(ks[13], (N_RWKV, D, RWKV_AAA_LORA), D ** -0.5),
        'rwkv_a2': nrm(ks[14], (N_RWKV, RWKV_AAA_LORA, D), RWKV_AAA_LORA ** -0.5),
        'rwkv_v0': nrm(ks[15], (N_RWKV - 1, D), 0.1),
        'rwkv_v1': nrm(ks[16], (N_RWKV - 1, D, RWKV_MV_LORA), D ** -0.5),
        'rwkv_v2': nrm(ks[17], (N_RWKV - 1, RWKV_MV_LORA, D), RWKV_MV_LORA ** -0.5),
        'rwkv_k_k': 0.85 + nrm(ks[18], (N_RWKV, D), 0.05),
        'rwkv_k_a': 1.0 + nrm(ks[19], (N_RWKV, D), 0.05),
        'rwkv_r_k': nrm(ks[20], (N_RWKV, RWKV_HEADS, RWKV_HEAD), 0.1),
        'rwkv_ln_w': 1.0 + nrm(ks[21], (N_RWKV, D), 0.02),
        'rwkv_ln_b': nrm(ks[22], (N_RWKV, D), 0.01),
        'rwkv_w_o': nrm(ks[23], (N_RWKV, D, D), D ** -0.5),
        'hgrn_w_in': nrm(ks[24], (N_HGRN, D, 4 * D), D ** -0.5),
        'hgrn_lb_logits': nrm(ks[25], (N_HGRN, HGRN_HEADS * HGRN_DK), 0.5),
        'hgrn_norm_w': 1.0 + nrm(ks[26], (N_HGRN, HGRN_DV), 0.02),
        'hgrn_w_o': nrm(ks[27], (N_HGRN, D, D), D ** -0.5),
    }

def reference(x_prompt, x_sample, state_rwkv_shift, state_rwkv_wkv, state_hgrn,
              norm_pre, norm_post, rwkv_mu, rwkv_w_in, rwkv_w0, rwkv_w1, rwkv_w2,
              rwkv_a0, rwkv_a1, rwkv_a2, rwkv_v0, rwkv_v1, rwkv_v2, rwkv_k_k, rwkv_k_a,
              rwkv_r_k, rwkv_ln_w, rwkv_ln_b, rwkv_w_o, hgrn_w_in, hgrn_lb_logits,
              hgrn_norm_w, hgrn_w_o):
    lb_soft = jax.nn.softmax(hgrn_lb_logits.astype(jnp.float32), axis=0)
    lower_bounds = jnp.cumsum(lb_soft, axis=0) - lb_soft[0]

    def trunk(x, shift0, wkv0, hgrn0):
        shifts, wkvs, hgrns = [], [], []
        v_first = None
        for layer in range(DEPTH):
            j = layer // N_MIXERS
            h = rms_norm(x, norm_pre[layer])
            if layer % N_MIXERS == 0:
                vres = None if j == 0 else (rwkv_v0[j - 1], rwkv_v1[j - 1], rwkv_v2[j - 1])
                out, sh, st, v_first = rwkv7_mix(
                    h, shift0[j], wkv0[j], v_first, vres, rwkv_mu[j], rwkv_w_in[j],
                    rwkv_w0[j], rwkv_w1[j], rwkv_w2[j], rwkv_a0[j], rwkv_a1[j], rwkv_a2[j],
                    rwkv_k_k[j], rwkv_k_a[j], rwkv_r_k[j], rwkv_ln_w[j], rwkv_ln_b[j], rwkv_w_o[j])
                shifts.append(sh.astype(x.dtype))
                wkvs.append(st.astype(x.dtype))
            else:
                out, st = hgrn2_mix(h, hgrn0[j], lower_bounds[j], hgrn_w_in[j], hgrn_norm_w[j], hgrn_w_o[j])
                hgrns.append(st.astype(x.dtype))
            x = x + rms_norm(out, norm_post[layer])
        return x, jnp.stack(shifts), jnp.stack(wkvs), jnp.stack(hgrns)

    B = x_prompt.shape[0]
    dt = x_prompt.dtype
    zero_shift = jnp.zeros((N_RWKV, B, D_MODEL), dt)
    zero_wkv = jnp.zeros((N_RWKV, B, RWKV_HEADS, RWKV_HEAD, RWKV_HEAD), dt)
    zero_hgrn = jnp.zeros((N_HGRN, B, HGRN_HEADS, HGRN_DK, HGRN_DV), dt)
    y_prompt, p_shift, p_wkv, p_hgrn = trunk(x_prompt, zero_shift, zero_wkv, zero_hgrn)
    y_sample, s_shift, s_wkv, s_hgrn = trunk(x_sample, state_rwkv_shift, state_rwkv_wkv, state_hgrn)
    return (y_prompt, y_sample, p_shift, p_wkv, p_hgrn, s_shift, s_wkv, s_hgrn)


_drawn_inputs = setup_inputs


def setup_inputs(seed=0):
    import zlib

    import numpy as np

    out = dict(_drawn_inputs(seed))
    spreads = {}
    factors = {'norm_post': 2.768,
     'rwkv_w1': 7.069,
     'rwkv_w2': 7.203,
     'rwkv_ln_w': 3.422,
     'rwkv_ln_b': 6.774,
     'hgrn_norm_w': 5.279}
    for name, (base, spread) in spreads.items():
        noise = np.random.default_rng([zlib.crc32(name.encode()), seed]).standard_normal(out[name].shape)
        drawn = base * np.exp(spread * noise) if base else spread * noise
        out[name] = __import__('jax').numpy.asarray(drawn.astype(out[name].dtype))
    for name, factor in factors.items():
        out[name] = (out[name] * factor).astype(out[name].dtype)
    return out
```

```python
from collections import namedtuple
from contextlib import ExitStack

import numpy as np

import concourse.bass as bass
from concourse import mybir

ALU = mybir.AluOpType
ACT = mybir.ActivationFunctionType
F32 = mybir.dt.float32
F32R = mybir.dt.float32r

P = 128
D = 2048
KT = D // P
SEQ = 512
NB, DS = 8, 4
SMP = NB * DS
T = SEQ + SMP
TH = T // 2
LORA = 96
HD = 64
C = 64
NCH = SEQ // C
NORM_EPS = 1e-6
GN_EPS = 1e-5 * HD
GATE_FLOOR = 1e-30
LN_SPLIT = 2.0 ** -50
KK_SCALE = 2.0 ** 20
DECAY = float(np.exp(np.float32(-0.5)))
RWKV_LEVELS = (1, 2, 4, 8, 16, 32)
HGRN_LEVELS = (1, 2, 4, 8, 16, 32)

PAR = ["pre0", "pre1", "post0", "post1", "mu0", "mu1", "mu2", "mu3", "mu4", "mu5", "w0", "a0",
       "k_k", "k_a", "r_k", "ln_w", "ln_b", "lb", "norm_w"]
NPAR = len(PAR)


def named(**got):
    return namedtuple("Named", list(got))(*got.values())


def par(params, name, kt):
    return params[:, kt, PAR.index(name):PAR.index(name) + 1]


def tile_of(t, i):
    return t[:, bass.ds(i, 1), :].rearrange("p a c -> p (a c)")


def dram_tile(t, i):
    return t[bass.ds(i, 1), :, :].rearrange("a p c -> p (a c)")


def halves(t):
    return t.rearrange("p (a c) -> p a c", a=2)


def recip_root(act, out, ms, scale, eps, ln_sem, out_sem, ln_at):
    act.activation(out, ms, ACT.Ln, scale=scale, bias=eps).then_inc(ln_sem, 1)
    act.wait_ge(ln_sem, ln_at)
    act.activation(out, out, ACT.Exp, scale=-0.5).then_inc(out_sem, 1)


class Region:

    def __init__(self, nc, ctx, tag):
        self.nc, self.ctx, self.tag = nc, ctx, tag

    def sb(self, name, shape, dt=F32):
        return self.ctx.enter_context(self.nc.sbuf_tensor(f"{self.tag}_{name}", shape, dt))

    def ps(self, name, shape):
        return self.ctx.enter_context(self.nc.psum_tensor(f"{self.tag}_{name}", shape, F32))

    def sems(self, names):
        got = {n: self.ctx.enter_context(self.nc.semaphore(f"{self.tag}_{n}")) for n in names.split()}

        def clear():
            with self.nc.Block() as block:
                @block.gpsimd
                def _(pool):
                    for sem in got.values():
                        pool.sem_clear(sem)

        self.ctx.callback(clear)
        return named(**got)


def dense_matmuls(pe, out, w_hi, w_lo, x_hi, x_lo):
    for kt in range(KT):
        hi = w_hi[:, kt * P:(kt + 1) * P]
        lo = w_lo[:, kt * P:(kt + 1) * P]
        for n, (w, x) in enumerate(((hi, x_hi), (hi, x_lo), (lo, x_hi))):
            for a in range(2):
                mm = pe.matmul(out[:, a, 0:TH], w, x[:, kt, a * TH:(a + 1) * TH],
                               start=(kt == 0 and n == 0), stop=(kt == KT - 1 and n == 2))
    return mm


def rwkv_dense(nc, keep, lora, d):
    with ExitStack() as ctx:
        R = Region(nc, ctx, "ab")
        sb, ps = R.sb, R.ps
        params, eps = keep.params, keep.eps
        ones = sb("ones", [P, P])
        h = sb("h", [P, KT, T])
        delta = sb("delta", [P, KT, T])
        x = delta
        shift = sb("shift", [P, KT, NB])
        last = sb("last", [P, KT, NB + 1])
        x_hi, x_lo = sb("x_hi", [P, KT, T], F32R), sb("x_lo", [P, KT, T], F32R)
        raw = [sb(f"raw{b}", [P, D]) for b in range(2)]
        w_hi = [sb(f"w_hi{b}", [P, D], F32R) for b in range(2)]
        w_lo = [sb(f"w_lo{b}", [P, D], F32R) for b in range(2)]
        w1 = [raw[n][:, 0:KT * LORA].rearrange("p (k l) -> p k l", l=LORA) for n in range(2)]
        mix = [sb(f"mix{b}", [P, T]) for b in range(2)]
        stage = [sb(f"stage{b}", [P, T]) for b in range(2)]
        sq = stage
        rstd = mix[0]
        pair = [ps(f"pair{b}", [P, 2, 512]) for b in range(4)]
        s = R.sems("const_in x_in shift_in w1_in sq_ready sq_used ln_ready rstd_ready h_ready delta_ready "
                   "last_ready last_out lora_mix lora_used lora_out mix_ready mix_hi mix_lo "
                   "raw_in0 raw_in1 raw_hi0 raw_hi1 raw_lo0 raw_lo1 tile_ready0 tile_ready1 "
                   "evac0 evac1 stored0 stored1")
        raw_in, raw_hi, raw_lo = [s.raw_in0, s.raw_in1], [s.raw_hi0, s.raw_hi1], [s.raw_lo0, s.raw_lo1]
        tile_ready, evac, stored = [s.tile_ready0, s.tile_ready1], [s.evac0, s.evac1], [s.stored0, s.stored1]
        NPRJ = 4
        PAIRS = KT // 2
        ALL = NPRJ * PAIRS
        block = ctx.enter_context(nc.Block())


        @block.sync
        def _(sp):
            sp.dma_start(ones[:, :], keep.const("ones")).then_inc(s.const_in, 16)
            sp.dma_start(eps[:, :], keep.const("eps")).then_inc(s.const_in, 16)
            sp.dma_start(params[:, :, :], d.params).then_inc(s.const_in, 16)
            for q in range(4):
                sp.dma_start(x[:, 4 * q:4 * q + 4, :],
                             d.xT[4 * q:4 * q + 4].rearrange("k p c -> p k c")).then_inc(s.x_in, 16)
            sp.dma_start(shift[:, :, :], d.shiftT).then_inc(s.shift_in, 16)
            for n in range(2):
                sp.dma_start(w1[n], d.w1[n]).then_inc(s.w1_in, 16)
            sp.wait_ge(s.lora_used, 2 * KT)
            with sp.Fori(0, ALL) as i:
                for b in range(2):
                    sp.wait_ge(raw_hi[b], i + 1)
                    sp.wait_ge(raw_lo[b], i + 1)
                    sp.dma_start(raw[b][:, :], dram_tile(d.w_in, 2 * i + b)).then_inc(raw_in[b], 16)
            sp.wait_ge(s.last_ready, 2)
            sp.dma_start(d.last, last[:, :, :]).then_inc(s.last_out, 16)
            sp.wait_ge(s.last_out, 16)

        @block.tensor
        def _(pe):
            pe.wait_ge(s.const_in, 48)
            for b in range(2):
                pe.sem_inc(tile_ready[b], 1)
            for kt in range(KT):
                pe.wait_ge(s.sq_ready, kt + 1)
                for a in range(2):
                    mm = pe.matmul(pair[0][:, a, 0:TH], ones[:, :], sq[kt % 2][:, a * TH:(a + 1) * TH],
                                   start=(kt == 0), stop=(kt == KT - 1))
                mm.then_inc(s.sq_used, 1)
            pe.wait_ge(s.w1_in, 32)
            for n in range(2):
                for kt in range(KT):
                    pe.wait_ge(s.lora_mix, n * KT + kt + 1)
                    for a in range(2):
                        mm = pe.matmul(pair[1 + n][0:LORA, a, 0:TH], w1[n][:, kt, :],
                                       mix[kt % 2][:, a * TH:(a + 1) * TH],
                                       start=(kt == 0), stop=(kt == KT - 1))
                    mm.then_inc(s.lora_used, 1)
            pe.wait_ge(s.lora_out, 2)
            for n in range(NPRJ):
                pe.wait_ge(s.mix_lo, KT * (n + 1))
                with pe.Fori(0, PAIRS) as i:
                    for b in range(2):
                        pe.wait_ge(raw_hi[b], i + (n * PAIRS + 2))
                        pe.wait_ge(raw_lo[b], i + (n * PAIRS + 2))
                        pe.wait_ge(evac[b], i + (n * PAIRS + 1))
                        dense_matmuls(pe, pair[b], w_hi[b], w_lo[b], x_hi, x_lo).then_inc(tile_ready[b], 1)

        @block.scalar
        def _(act):
            for b in range(2):
                act.sem_inc(raw_hi[b], 1)
                act.sem_inc(evac[b], 1)
                act.sem_inc(stored[b], 16)
            act.wait_ge(s.x_in, 64)
            act.wait_ge(s.const_in, 48)
            for kt in range(KT):
                if kt >= 2:
                    act.wait_ge(s.sq_used, kt - 1)
                act.activation(sq[kt % 2][:, :], x[:, kt, :], ACT.Square).then_inc(s.sq_ready, 1)
            act.wait_ge(s.sq_used, KT)
            recip_root(act, halves(rstd[:, :]), pair[0][:, :, 0:TH], 1.0 / D, eps[:, 0:1],
                       s.ln_ready, s.rstd_ready, 1)
            for n in range(2):
                act.wait_ge(s.lora_used, (n + 1) * KT)
                func = (ACT.Tanh, ACT.Copy)[n]
                act.activation(halves(lora[n][:, :]), pair[1 + n][0:LORA, :, 0:TH], func).then_inc(s.lora_out, 1)

            def split_hi(b, j):
                act.wait_ge(raw_in[b], 16 * (j + 1))
                act.wait_ge(tile_ready[b], j + 1)
                act.copy(w_hi[b][:, :], raw[b][:, :]).then_inc(raw_hi[b], 1)

            def evacuate(b, j, n, m):
                act.wait_ge(tile_ready[b], j + 2)
                act.wait_ge(stored[b], 16 * (j + 1))
                act.copy(halves(stage[b][:, :]), pair[b][:, :, 0:TH]).then_inc(evac[b], 1)
                act.wait_ge(evac[b], j + 2)
                act.dma_start(dram_tile(d.rkvz[n], m), stage[b][:, :]).then_inc(stored[b], 16)

            for b in range(2):
                split_hi(b, 0)
            for n in range(NPRJ):
                for kt in range(KT):
                    act.wait_ge(s.mix_ready, n * KT + kt + 1)
                    act.copy(x_hi[:, kt, :], mix[kt % 2][:, :]).then_inc(s.mix_hi, 1)
                last_pair = n == NPRJ - 1
                with act.Fori(0, PAIRS - last_pair) as i:
                    for b in range(2):
                        evacuate(b, i + n * PAIRS, n, 2 * i + b)
                        split_hi(b, i + (n * PAIRS + 1))
                if last_pair:
                    for b in range(2):
                        evacuate(b, ALL - 1, n, KT - 2 + b)
            for b in range(2):
                act.wait_ge(stored[b], 16 * (ALL + 1))

        @block.vector
        def _(dve):
            for b in range(2):
                dve.sem_inc(raw_lo[b], 1)
            dve.wait_ge(s.rstd_ready, 1)
            for kt in range(KT):
                dve.scalar_tensor_tensor(h[:, kt, :], x[:, kt, :], par(params, "pre0", kt), rstd[:, :],
                                         ALU.mult, ALU.mult).then_inc(s.h_ready, 1)
            dve.wait_ge(s.h_ready, KT)
            dve.tensor_copy(last[:, :, 0:1], h[:, :, SEQ - 1:SEQ]).then_inc(s.last_ready, 1)
            dve.tensor_copy(last[:, :, 1:], h[:, :, SEQ + DS - 1:T:DS]).then_inc(s.last_ready, 1)
            dve.wait_ge(s.shift_in, 16)
            dve.tensor_scalar(delta[:, :, 0:1], h[:, :, 0:1], -1.0, None, ALU.mult).then_inc(s.delta_ready, 1)
            dve.tensor_tensor(delta[:, :, 1:SEQ], h[:, :, 0:SEQ - 1], h[:, :, 1:SEQ],
                              ALU.subtract).then_inc(s.delta_ready, 1)
            smp, dsm = h[:, :, SEQ:T], delta[:, :, SEQ:T]
            dve.tensor_tensor(dsm[:, :, 0:SMP:DS], shift[:, :, :], smp[:, :, 0:SMP:DS],
                              ALU.subtract).then_inc(s.delta_ready, 1)
            for j in range(1, DS):
                dve.tensor_tensor(dsm[:, :, j:SMP:DS], smp[:, :, j - 1:SMP:DS], smp[:, :, j:SMP:DS],
                                  ALU.subtract).then_inc(s.delta_ready, 1)
            dve.wait_ge(s.delta_ready, 3 + DS - 1)

            def blend(kt, which):
                return dve.scalar_tensor_tensor(mix[kt % 2][:, :], delta[:, kt, :], par(params, which, kt),
                                                h[:, kt, :], ALU.mult, ALU.add)

            for n in range(2):
                for kt in range(KT):
                    if n * KT + kt >= 2:
                        dve.wait_ge(s.lora_used, n * KT + kt - 1)
                    blend(kt, f"mu{4 + n}").then_inc(s.lora_mix, 1)
            dve.wait_ge(s.lora_used, 2 * KT)

            def split_lo(b, j):
                dve.wait_ge(raw_hi[b], j + 2)
                dve.wait_ge(tile_ready[b], j + 1)
                dve.tensor_tensor(w_lo[b][:, :], raw[b][:, :], w_hi[b][:, :].bitcast(F32),
                                  ALU.subtract).then_inc(raw_lo[b], 1)

            for b in range(2):
                split_lo(b, 0)
            for n in range(NPRJ):
                if n:
                    for b in range(2):
                        dve.wait_ge(tile_ready[b], n * PAIRS + 1)
                for kt in range(KT + 1):
                    if kt < KT:
                        if n * KT + kt >= 2:
                            dve.wait_ge(s.mix_lo, n * KT + kt - 1)
                        blend(kt, f"mu{n}").then_inc(s.mix_ready, 1)
                    if kt:
                        dve.wait_ge(s.mix_hi, n * KT + kt)
                        dve.tensor_tensor(x_lo[:, kt - 1, :], mix[(kt - 1) % 2][:, :],
                                          x_hi[:, kt - 1, :].bitcast(F32), ALU.subtract).then_inc(s.mix_lo, 1)
                with dve.Fori(0, PAIRS - (n == NPRJ - 1)) as i:
                    for b in range(2):
                        split_lo(b, i + (n * PAIRS + 1))


def out_dense(nc, keep, d, tag, w_out, x_src, post, pre_next):
    with ExitStack() as ctx:
        R = Region(nc, ctx, tag)
        sb, ps = R.sb, R.ps
        params, eps = keep.params, keep.eps
        ones = sb("ones", [P, P])
        x_hi, x_lo = sb("x_hi", [P, KT, T], F32R), sb("x_lo", [P, KT, T], F32R)
        raw = [sb(f"raw{b}", [P, D]) for b in range(2)]
        w_hi = [sb(f"w_hi{b}", [P, D], F32R) for b in range(2)]
        w_lo = [sb(f"w_lo{b}", [P, D], F32R) for b in range(2)]
        y = [sb(f"y{b}", [P, T]) for b in range(3)]
        o = sb("o", [P, KT, T])
        x = [sb(f"x{b}", [P, T]) for b in range(3)]
        sq = [sb(f"sq{b}", [P, T]) for b in range(2)]
        rstd = sb("rstd", [P, T])
        pair = [ps(f"pair{b}", [P, 2, 512]) for b in range(4)]
        s = R.sems("const_in y_in0 y_in1 y_in2 y_hi y_lo sq_ready sq_used ln_ready rstd_ready scaled x_ready "
                   "x_in0 x_in1 x_in2 x_out0 x_out1 x_out2 "
                   "h_ready h_out "
                   "raw_in0 raw_in1 raw_hi0 raw_hi1 raw_lo0 raw_lo1 tile_ready0 tile_ready1 evac0 evac1")
        raw_in, raw_hi, raw_lo = [s.raw_in0, s.raw_in1], [s.raw_hi0, s.raw_hi1], [s.raw_lo0, s.raw_lo1]
        tile_ready, evac = [s.tile_ready0, s.tile_ready1], [s.evac0, s.evac1]
        PAIRS = KT // 2
        y_in, x_in = [s.y_in0, s.y_in1, s.y_in2], [s.x_in0, s.x_in1, s.x_in2]
        x_out = [s.x_out0, s.x_out1, s.x_out2]
        x_next = d.x1 if pre_next else d.y_out
        block = ctx.enter_context(nc.Block())

        @block.sync
        def _(sp):
            sp.dma_start(ones[:, :], keep.const("ones")).then_inc(s.const_in, 16)
            for kt in range(KT):
                if kt == 2:
                    for b in range(2):
                        sp.dma_start(raw[b][:, :], w_out[b]).then_inc(raw_in[b], 16)
                if kt >= 3:
                    sp.wait_ge(s.y_lo, kt - 2)
                sp.dma_start(y[kt % 3][:, :], d.yz[kt]).then_inc(y_in[kt % 3], 16)
            with sp.Fori(0, PAIRS - 1) as i:
                for b in range(2):
                    sp.wait_ge(raw_hi[b], i + 2)
                    sp.wait_ge(raw_lo[b], i + 2)
                    sp.dma_start(raw[b][:, :], dram_tile(w_out, 2 * i + (2 + b))).then_inc(raw_in[b], 16)
            for kt in range(KT):
                if kt >= 3:
                    sp.wait_ge(x_out[kt % 3], 16 * (kt // 3))
                sp.dma_start(x[kt % 3][:, :], x_src[kt]).then_inc(x_in[kt % 3], 16)
            if pre_next:
                for kt in range(KT):
                    sp.wait_ge(s.h_ready, kt + 1)
                    sp.dma_start(d.h1[kt], o[:, kt, :]).then_inc(s.h_out, 16)
                sp.wait_ge(s.h_out, 16 * KT)

        @block.tensor
        def _(pe):
            for b in range(2):
                pe.sem_inc(tile_ready[b], 1)
            pe.wait_ge(s.y_lo, KT)
            with pe.Fori(0, PAIRS) as i:
                for b in range(2):
                    pe.wait_ge(raw_hi[b], i + 2)
                    pe.wait_ge(raw_lo[b], i + 2)
                    pe.wait_ge(evac[b], i + 1)
                    dense_matmuls(pe, pair[b], w_hi[b], w_lo[b], x_hi, x_lo).then_inc(tile_ready[b], 1)
            pe.wait_ge(s.const_in, 16)
            for q in range(1 + bool(pre_next)):
                for kt in range(KT):
                    pe.wait_ge(s.sq_ready, q * KT + kt + 1)
                    for a in range(2):
                        mm = pe.matmul(pair[2 + q][:, a, 0:TH], ones[:, :], sq[kt % 2][:, a * TH:(a + 1) * TH],
                                       start=(kt == 0), stop=(kt == KT - 1))
                    mm.then_inc(s.sq_used, 1)

        @block.scalar
        def _(act):
            for b in range(2):
                act.sem_inc(raw_hi[b], 1)
                act.sem_inc(evac[b], 1)

            def split_hi(b, j):
                act.wait_ge(raw_in[b], 16 * (j + 1))
                act.wait_ge(tile_ready[b], j + 1)
                act.copy(w_hi[b][:, :], raw[b][:, :]).then_inc(raw_hi[b], 1)

            def evacuate(b, j):
                act.wait_ge(tile_ready[b], j + 2)
                act.copy(halves(tile_of(o, 2 * j + b)), pair[b][:, :, 0:TH]).then_inc(evac[b], 1)

            for kt in range(KT):
                act.wait_ge(y_in[kt % 3], 16 * (kt // 3 + 1))
                act.copy(x_hi[:, kt, :], y[kt % 3][:, :]).then_inc(s.y_hi, 1)
            for b in range(2):
                split_hi(b, 0)
            with act.Fori(0, PAIRS - 1) as i:
                for b in range(2):
                    evacuate(b, i)
                    split_hi(b, i + 1)
            for b in range(2):
                act.wait_ge(tile_ready[b], PAIRS + 1)
                act.copy(halves(o[:, KT - 2 + b, :]), pair[b][:, :, 0:TH]).then_inc(evac[b], 1)
            for b in range(2):
                act.wait_ge(evac[b], PAIRS + 1)
            for q in range(1 + bool(pre_next)):
                for kt in range(KT):
                    if q:
                        act.wait_ge(s.x_ready, kt + 1)
                    if q * KT + kt >= 2:
                        act.wait_ge(s.sq_used, q * KT + kt - 1)
                    act.activation(sq[kt % 2][:, :], o[:, kt, :], ACT.Square).then_inc(s.sq_ready, 1)
                act.wait_ge(s.sq_used, (q + 1) * KT)
                if q:
                    act.wait_ge(s.x_ready, KT)
                recip_root(act, halves(rstd[:, :]), pair[2 + q][:, :, 0:TH], 1.0 / D, eps[:, 0:1],
                           s.ln_ready, s.rstd_ready, q + 1)

        @block.gpsimd
        def _(pool):
            for kt in range(KT):
                pool.wait_ge(s.x_ready, kt + 1)
                pool.dma_start(x_next[kt], x[kt % 3][:, :]).then_inc(x_out[kt % 3], 16)
            for b in range(3):
                pool.wait_ge(x_out[b], 16 * len(range(b, KT, 3)))

        @block.vector
        def _(dve):
            for b in range(2):
                dve.sem_inc(raw_lo[b], 1)

            def split_lo(b, j):
                dve.wait_ge(raw_hi[b], j + 2)
                dve.wait_ge(tile_ready[b], j + 1)
                dve.tensor_tensor(w_lo[b][:, :], raw[b][:, :], w_hi[b][:, :].bitcast(F32),
                                  ALU.subtract).then_inc(raw_lo[b], 1)

            for kt in range(KT):
                dve.wait_ge(s.y_hi, kt + 1)
                dve.tensor_tensor(x_lo[:, kt, :], y[kt % 3][:, :], x_hi[:, kt, :].bitcast(F32),
                                  ALU.subtract).then_inc(s.y_lo, 1)
            for b in range(2):
                split_lo(b, 0)
            with dve.Fori(0, PAIRS - 1) as i:
                for b in range(2):
                    split_lo(b, i + 1)
            dve.wait_ge(s.rstd_ready, 1)
            for kt in range(KT):
                dve.scalar_tensor_tensor(o[:, kt, :], o[:, kt, :], par(params, post, kt), rstd[:, :],
                                         ALU.mult, ALU.mult).then_inc(s.scaled, 1)
                dve.wait_ge(s.scaled, 2 * kt + 1)
                dve.wait_ge(x_in[kt % 3], 16 * (kt // 3 + 1))
                dve.tensor_tensor(o[:, kt, :], o[:, kt, :], x[kt % 3][:, :], ALU.add).then_inc(s.scaled, 1)
                dve.wait_ge(s.scaled, 2 * kt + 2)
                dve.tensor_copy(x[kt % 3][:, :], o[:, kt, :]).then_inc(s.x_ready, 1)
            if pre_next:
                dve.wait_ge(s.rstd_ready, 2)
                for kt in range(KT):
                    dve.scalar_tensor_tensor(o[:, kt, :], o[:, kt, :], par(params, pre_next, kt), rstd[:, :],
                                             ALU.mult, ALU.mult).then_inc(s.h_ready, 1)


def rwkv_recurrence(nc, keep, lora, d):
    with ExitStack() as ctx:
        R = Region(nc, ctx, "c")
        sb, ps = R.sb, R.ps
        params, eps = keep.params, keep.eps
        NL = len(RWKV_LEVELS)
        names = ["ident", "bones", "bmean", "strict", "lev1n", "eye4", "incl", "s_mask", "s_lev1", "s_lev2",
                 "s_lev1n", "s_eye", "s_seq", "reset"] + [f"lev{m}" for m in RWKV_LEVELS]
        tables = {n: sb(f"k_{n}", [P, keep.col[n][1]]) for n in names}
        k = named(**tables)
        lev = [sb_ for sb_ in (k.lev1, k.lev2, k.lev4, k.lev8, k.lev16, k.lev32)]
        rt, kt_, vt, zt = (sb(f"{n}t", [P, T]) for n in "rkvz")
        parm = sb("parm", [P, NPAR])
        w2 = sb("w2", [LORA, 2, P])
        vE, vEs = sb("vE", [P, NCH, P]), sb("vEs", [P, 2 * SMP])
        SEs, Sc = sb("SEs", [P, NB, P]), sb("Sc", [P, NB, HD])
        e3, mn3, sg3 = (sb(n, [P, 3, T]) for n in ("e3", "mn3", "sg3"))
        cs, csx, W, Wi, Wp = (sb(n, [P, T]) for n in ("cs", "csx", "W", "Wi", "Wp"))
        ksq, ssm, rn, kkn, bb, kf, k2, rk, bv, zs, rho = (
            sb(n, [P, T]) for n in ("ksq", "ssm", "rn", "kkn", "bb", "kf", "k2", "rk", "bv", "zs", "rho"))
        aE, bE, kE = (sb(n, [P, NCH, P]) for n in ("aE", "bE", "kE"))
        bEs, kEs = sb("bEs", [P, 2 * SMP]), sb("kEs", [P, 2 * SMP])
        arS = sb("arS", [P, 3 * SMP])
        aEs, rhoS = arS[:, 0:2 * SMP], arS[:, 2 * SMP:3 * SMP]
        bds, kds = sb("bds", [P, 2 * SMP]), sb("kds", [P, 2 * SMP])
        Mab, Mak = sb("Mab", [P, NCH, P]), sb("Mak", [P, NCH, P])
        Mlev = [sb(f"Mlev{m}", [P, NCH, P]) for m in RWKV_LEVELS]
        Mrb, Mrk = sb("Mrb", [P, NCH, C]), sb("Mrk", [P, NCH, C])
        Ti, TiT, X = (sb(n, [P, NCH, P]) for n in ("Ti", "TiT", "X"))
        btok, ktok, vtok = (sb(n, [P, NCH, P]) for n in ("btok", "ktok", "vtok"))
        Rc, Uc, SE = (sb(n, [P, P]) for n in ("Rc", "Uc", "SE"))
        ybuf = sb("ybuf", [P, T])
        S2 = 2 * SMP
        Ms = sb("Ms", [S2, 2, 3 * SMP])
        Tis, TiTs, M1s, M2s, Xs = (sb(n, [S2, S2]) for n in ("Tis", "TiTs", "M1s", "M2s", "Xs"))
        toks = sb("toks", [S2, 3, P])
        RTs, Rs, Us = sb("RTs", [P, S2]), sb("Rs", [S2, P]), sb("Us", [S2, P])
        Um, Vm = sb("Um", [S2, NB, HD]), sb("Vm", [S2, NB, HD])
        sdec, snew, sfin = sb("sdec", [P, NB, HD]), sb("snew", [P, NB, HD]), sb("sfin", [P, HD])
        pA, pB = ps("pA", [P, 2, 512]), ps("pB", [P, 2, 512])
        A = [pA[:, 0, :], pA[:, 1, :]]
        B = [pB[:, 0, :], pB[:, 1, :]]
        bank = [ps(f"bank{n}", [P, 512]) for n in range(4)]
        X_ps, Y_ps, YT_ps = [bank[0], bank[1]], [bank[2], bank[3]], A
        y_ps, S_ps, R_ps, U_ps = bank[0][:, :], bank[1][:, 0:P], bank[2][:, 0:P], bank[3][:, 0:P]
        s = R.sems("vm_all passed const_in zeroed loaded stored "
                   "lora_mm abs_r exp3 ln3 min3 ls3 sg3 scan csx decays ksq ss_mm ssm lnk rn kkn bb kf k2 rk "
                   "bonus_mm bv zs expand expand_pool bds kds "
                   "mab_mm mabn_mm mak_mm mrb_mm mrk_mm mab makd mrbd mrkd ti_lev ti0 lev_r tit0 "
                   "tok_mm tok_ev x_mm x_ev y_mm ti_r yt_mm tit_r "
                   "r_mm r_ev u_mm u_ev s_mm s_ev yc_mm "
                   "sm_mm sms smt smd smt0 stok_mm stok_ev sx_mm sx_ev syt_mm stit "
                   "srt_mm srt_ev sr_mm sr_ev su_mm su_ev sy_mm um vm sd_mm sdec snew sfin "
                   "y_ev mean_mm yc ysq var_mm gln grs yn yw yb yz")
        LOADS = 14
        block = ctx.enter_context(nc.Block())

        def col_of(name):
            return parm[:, PAR.index(name):PAR.index(name) + 1]

        def half(t, hh, n=P):
            return t[n // 2 * hh:n // 2 * (hh + 1)]

        def prompt(t, hh):
            return t[64 * hh:64 * hh + 64, 0:SEQ].rearrange("p (c t) -> p c t", t=C)

        def chunk(t, c):
            return t[:, c * C:(c + 1) * C]

        @block.sync
        def _(sp):
            for n in names:
                sp.dma_start(tables[n][:, :], keep.const(n)).then_inc(s.const_in, 16)
            sp.wait_ge(s.zeroed, 6)

            def loads(i):
                for n, t in enumerate((rt, kt_, vt, zt)):
                    sp.dma_start(t[:, :], dram_tile(d.rkvz[n], i)).then_inc(s.loaded, 16)
                sp.dma_start(w2[:, 0, :], dram_tile(d.w2[0], i)).then_inc(s.loaded, 16)
                sp.dma_start(w2[:, 1, :], dram_tile(d.w2[1], i)).then_inc(s.loaded, 16)
                for hh in range(2):
                    rows = slice(64 * hh, 64 * hh + 64)
                    src = d.rkvz[2][bass.ds(i, 1), rows, :]
                    sp.dma_start(vE[rows, :, rows], src[:, :, 0:SEQ].rearrange("a p (c t) -> p (a c) t", t=C)
                                 ).then_inc(s.loaded, 16)
                    sp.dma_start(vEs[rows, SMP * hh:SMP * hh + SMP], src[:, :, SEQ:T].rearrange("a p c -> p (a c)")
                                 ).then_inc(s.loaded, 16)
                    sp.dma_start(SEs[rows, :, rows], d.wkv[bass.ds(i, 1), rows, :, :].rearrange(
                        "a p b v -> p (a b) v")).then_inc(s.loaded, 16)
                sp.dma_start(Sc[:, :, :], d.wkv[bass.ds(i, 1), :, :, :].rearrange("a p b v -> p (a b) v")
                             ).then_inc(s.loaded, 16)

            def parameters(i):
                sp.dma_start(parm[:, :], tile_of(d.params, i)).then_inc(s.loaded, 16)

            def states_out(i):
                sp.wait_ge(s.snew, i + 1)
                sp.dma_start(d.wkv_s[bass.ds(i, 1), :, :, :].rearrange("a p b v -> p (a b) v"),
                             snew[:, :, :]).then_inc(s.stored, 16)
                sp.wait_ge(s.sfin, 2 * i + 2)
                sp.dma_start(dram_tile(d.wkv_p, i), sfin[:, :]).then_inc(s.stored, 16)

            def output(i):
                sp.wait_ge(s.yz, i + 1)
                sp.dma_start(dram_tile(d.yz, i), ybuf[:, :]).then_inc(s.stored, 16)
                sp.wait_ge(s.stored, 48 * i + 48)

            loads(0)
            parameters(0)
            with sp.Fori(0, KT - 1) as i:
                states_out(i)
                loads(i + 1)
                output(i)
                parameters(i + 1)
            states_out(KT - 1)
            output(KT - 1)

        def over_halves(pe, out, lhsT, rhs):
            for a in range(2):
                mm = pe.matmul(out[:, a, 0:TH], lhsT, rhs[:, a * TH:(a + 1) * TH], start=True, stop=True)
            return mm

        @block.tensor
        def _(pe):
            pe.wait_ge(s.const_in, 16 * len(names))
            with pe.Fori(0, KT) as i:
                pe.wait_ge(s.loaded, (i + 1) * (16 * LOADS))
                over_halves(pe, pA, w2[:, 0, :], lora[0])
                over_halves(pe, pB, w2[:, 1, :], lora[1]).then_inc(s.lora_mm, 1)
                pe.wait_ge(s.ksq, i + 1)
                pe.wait_ge(s.min3, 3 * i + 3)
                pe.wait_ge(s.abs_r, 3 * i + 3)
                over_halves(pe, pA, k.bones[:, :], ksq).then_inc(s.ss_mm, 1)
                pe.wait_ge(s.rk, i + 1)
                over_halves(pe, pB, k.bones[:, :], rk).then_inc(s.bonus_mm, 1)
                pe.wait_ge(s.expand, 10 * i + 10)
                pe.wait_ge(s.expand_pool, 4 * i + 4)
                for g in range(2):
                    for q in range(4):
                        c = 4 * g + q
                        mm = pe.matmul(bank[g][:, q * P:(q + 1) * P], bE[:, c, :], aE[:, c, :], start=True, stop=True)
                    mm.then_inc(s.mab_mm, 1)
                for g in range(2):
                    for q in range(4):
                        c = 4 * g + q
                        mm = pe.matmul(bank[2 + g][:, q * P:(q + 1) * P], aE[:, c, :], bE[:, c, :], start=True, stop=True)
                    mm.then_inc(s.mabn_mm, 1)
                pe.wait_ge(s.ssm, i + 1)
                for g in range(2):
                    for q in range(4):
                        c = 4 * g + q
                        mm = pe.matmul(A[g][:, q * P:(q + 1) * P], kE[:, c, :], aE[:, c, :], start=True, stop=True)
                    mm.then_inc(s.mak_mm, 1)
                pe.wait_ge(s.bv, i + 1)
                for c in range(NCH):
                    mm = pe.matmul(chunk(B[0], c), bE[:, c, :], chunk(rho, c), start=True, stop=True)
                mm.then_inc(s.mrb_mm, 1)
                for c in range(NCH):
                    mm = pe.matmul(chunk(B[1], c), kE[:, c, :], chunk(rho, c), start=True, stop=True)
                mm.then_inc(s.mrk_mm, 1)
                n = 0
                for src in (bE, kE, vE):
                    for g in range(2):
                        if n == 0:
                            pe.wait_ge(s.mab, 2 * i + 1)
                        if n == 1:
                            pe.wait_ge(s.mab, 2 * i + 2)
                        if n in (2, 3):
                            pe.wait_ge(s.ti_lev, 2 * i + n - 1)
                        if n >= 4:
                            pe.wait_ge(s.tok_ev, 6 * i + n - 3)
                        for q in range(4):
                            mm = pe.transpose(bank[n % 4][:, q * P:(q + 1) * P], src[:, 4 * g + q, :], k.ident[:, :])
                        mm.then_inc(s.tok_mm, 1)
                        n += 1
                pe.wait_ge(s.tok_ev, 6 * i + 6)
                pe.wait_ge(s.ti0, 2 * i + 2)
                pe.wait_ge(s.tit0, i + 1)
                pe.wait_ge(s.makd, 2 * i + 2)
                for l in range(1, NL):
                    pe.wait_ge(s.lev_r, 6 * i + l + 1)
                    for g in range(2):
                        if l > 1:
                            pe.wait_ge(s.ti_r, 8 * i + 2 * (l - 2) + g + 1)
                        for q in range(4):
                            c = 4 * g + q
                            mm = pe.matmul(X_ps[g][:, q * P:(q + 1) * P], Mlev[l][:, c, :], Ti[:, c, :],
                                           start=True, stop=True)
                        mm.then_inc(s.x_mm, 1)
                    for g in range(2):
                        pe.wait_ge(s.x_ev, 10 * i + 2 * (l - 1) + g + 1)
                        if l > 1:
                            pe.wait_ge(s.tit_r, 10 * i + 2 * (l - 2) + g + 1)
                        if l < NL - 1:
                            for q in range(4):
                                c = 4 * g + q
                                mm = pe.matmul(Y_ps[g][:, q * P:(q + 1) * P], TiT[:, c, :], X[:, c, :],
                                               start=True, stop=True)
                            mm.then_inc(s.y_mm, 1)
                        for q in range(4):
                            c = 4 * g + q
                            mm = pe.matmul(YT_ps[g][:, q * P:(q + 1) * P], X[:, c, :], TiT[:, c, :],
                                           start=True, stop=True)
                        mm.then_inc(s.yt_mm, 1)
                pe.wait_ge(s.mrbd, i + 1)
                pe.wait_ge(s.mrkd, i + 1)
                pe.wait_ge(s.tit_r, 10 * i + 10)

                def sample(step):
                    if step == 0:
                        pe.wait_ge(s.bds, i + 1)
                        pe.wait_ge(s.kds, i + 1)
                        pe.matmul(A[0][0:S2, 0:96], bEs[:, :], arS[:, :], start=True, stop=True)
                        pe.matmul(A[0][0:S2, 96:192], kEs[:, :], arS[:, :], start=True, stop=True)
                        pe.matmul(A[0][0:S2, 192:256], aEs, bEs[:, :], start=True, stop=True).then_inc(s.sm_mm, 1)
                    if step == 1:
                        pe.sem_inc(s.passed, 1)
                        for n, src in enumerate((vEs, bds, kds)):
                            mm = pe.transpose(A[1][0:S2, n * P:(n + 1) * P], src[:, :], k.ident[:, :])
                        mm.then_inc(s.stok_mm, 1)
                    if step == 2:
                        pe.wait_ge(s.smt0, 2 * i + 2)
                        pe.sem_inc(s.passed, 1)
                        pe.matmul(A[0][0:S2, 256:320], M2s[:, :], Tis[:, :], start=True, stop=True).then_inc(s.sx_mm, 1)
                    if step == 3:
                        pe.wait_ge(s.sx_ev, i + 1)
                        pe.sem_inc(s.passed, 1)
                        pe.matmul(A[0][0:S2, 320:384], Xs[:, :], TiTs[:, :], start=True, stop=True).then_inc(s.syt_mm, 1)
                    if step == 4:
                        pe.wait_ge(s.sms, i + 1)
                        pe.wait_ge(s.stok_ev, i + 1)
                        hb = "p (h t) -> p h t"
                        for b in range(NB):
                            cols = slice(DS * b, DS * b + DS)
                            pe.matmul(B[0][:, 0:S2].rearrange(hb, h=2)[:, :, cols], SEs[:, b, :],
                                      aEs.rearrange(hb, h=2)[:, :, cols],
                                      start=(b == 0), stop=False, skip_group_check=True)
                        mm = pe.matmul(B[0][:, 0:S2], toks[:, 0, :], Ms[:, 1, 0:S2], start=False, stop=True,
                                       skip_group_check=True)
                        mm.then_inc(s.srt_mm, 1)
                    if step == 5:
                        pe.wait_ge(s.srt_ev, i + 1)
                        pe.sem_inc(s.passed, 1)
                        pe.transpose(A[1][0:S2, 384:512], RTs[:, :], k.ident[:, :]).then_inc(s.sr_mm, 1)
                    if step == 6:
                        pe.wait_ge(s.sr_ev, i + 1)
                        pe.wait_ge(s.stit, i + 1)
                        pe.sem_inc(s.passed, 1)
                        pe.matmul(A[0][0:S2, 384:512], TiTs[:, :], Rs[:, :], start=True, stop=True).then_inc(s.su_mm, 1)
                    if step == 7:
                        pe.wait_ge(s.su_ev, i + 1)
                        for b in range(NB):
                            pe.matmul(B[0][:, 64 + DS * b:64 + DS * b + DS], SEs[:, b, :],
                                      rhoS[:, DS * b:DS * b + DS], start=(b == 0), stop=False, skip_group_check=True)
                        pe.matmul(B[0][:, 64:96], toks[:, 0, :], Ms[:, 1, S2:96], start=False, stop=False,
                                  skip_group_check=True)
                        mm = pe.matmul(B[0][:, 64:96], Us[:, :], Ms[:, 0, S2:96], start=False, stop=True,
                                       skip_group_check=True)
                        mm.then_inc(s.sy_mm, 1)
                    if step == 8:
                        pe.wait_ge(s.um, 2 * i + 2)
                        pe.wait_ge(s.vm, 2 * i + 2)
                        pe.matmul(B[1], toks[:, 2, :], Vm[:, :, :].rearrange("p b v -> p (b v)"), start=True, stop=False)
                        pe.matmul(B[1], toks[:, 1, :], Um[:, :, :].rearrange("p b v -> p (b v)"),
                                  start=False, stop=True).then_inc(s.sd_mm, 1)

                for c in range(NCH):
                    if c == 0:
                        pe.matmul(R_ps, Mak[:, c, :], vtok[:, c, :], start=True, stop=True).then_inc(s.r_mm, 1)
                    else:
                        pe.matmul(R_ps, Mak[:, c, :], vtok[:, c, :], start=True, stop=False)
                        pe.wait_ge(s.s_ev, 8 * i + c)
                        pe.matmul(R_ps, aE[:, c, :], SE[:, :], start=False, stop=True).then_inc(s.r_mm, 1)
                    pe.wait_ge(s.r_ev, 8 * i + c + 1)
                    pe.matmul(U_ps, TiT[:, c, :], Rc[:, :], start=True, stop=True).then_inc(s.u_mm, 1)
                    sample(c)
                    y_c = chunk(y_ps, c)
                    if c:
                        pe.matmul(y_c, SE[:, :], chunk(rho, c), start=True, stop=False)
                        pe.matmul(S_ps, k.ident[:, :], SE[:, :], start=True, stop=False)
                    pe.matmul(y_c, vtok[:, c, :], Mrk[:, c, :], start=(c == 0), stop=False)
                    pe.matmul(S_ps, ktok[:, c, :], vtok[:, c, :], start=(c == 0), stop=False)
                    pe.wait_ge(s.u_ev, 8 * i + c + 1)
                    pe.matmul(S_ps, btok[:, c, :], Uc[:, :], start=False, stop=True).then_inc(s.s_mm, 1)
                    pe.matmul(y_c, Uc[:, :], Mrb[:, c, :], start=False, stop=True).then_inc(s.yc_mm, 1)
                sample(8)
                pe.wait_ge(s.y_ev, 2 * i + 2)
                over_halves(pe, pA, k.bmean[:, :], ybuf).then_inc(s.mean_mm, 1)
                pe.wait_ge(s.ysq, i + 1)
                pe.wait_ge(s.snew, i + 1)
                over_halves(pe, pB, k.bmean[:, :], ksq).then_inc(s.var_mm, 1)

        @block.scalar
        def _(act):
            with act.Fori(0, KT) as i:
                act.wait_ge(s.loaded, (i + 1) * (16 * LOADS))
                act.activation(e3[:, 2, :], zt[:, :], ACT.Abs).then_inc(s.abs_r, 1)
                act.activation(ksq[:, :], kt_[:, :], ACT.Square, scale=col_of("k_k")).then_inc(s.ksq, 1)
                act.wait_ge(s.lora_mm, i + 1)
                act.activation(halves(e3[:, 0, :]), pA[:, :, 0:TH], ACT.Abs, bias=col_of("w0")).then_inc(s.abs_r, 1)
                act.activation(halves(e3[:, 1, :]), pB[:, :, 0:TH], ACT.Abs, bias=col_of("a0")).then_inc(s.abs_r, 1)
                act.wait_ge(s.abs_r, 3 * i + 3)
                act.activation(e3[:, :, :], e3[:, :, :], ACT.Exp, scale=-1.0).then_inc(s.exp3, 1)
                act.wait_ge(s.exp3, i + 1)
                act.activation(e3[:, :, :], e3[:, :, :], ACT.Ln, bias=1.0).then_inc(s.ln3, 1)
                act.wait_ge(s.ssm, i + 1)
                act.activation(rn[:, :], ssm[:, :], ACT.Ln, scale=KK_SCALE).then_inc(s.lnk, 1)
                act.wait_ge(s.lnk, i + 1)
                act.activation(rn[:, :], rn[:, :], ACT.Exp, scale=-0.5, bias=eps[:, 2:3]).then_inc(s.rn, 1)
                act.wait_ge(s.ls3, i + 1)
                act.activation(sg3[:, :, :], mn3[:, :, :], ACT.Exp).then_inc(s.sg3, 1)
                act.wait_ge(s.scan, i + 1)
                act.activation(W[:, :], cs[:, :], ACT.Exp, scale=-DECAY).then_inc(s.decays, 1)
                act.activation(Wi[:, :], cs[:, :], ACT.Exp, scale=DECAY).then_inc(s.decays, 1)
                act.wait_ge(s.csx, i + 1)
                act.activation(Wp[:, :], csx[:, :], ACT.Exp, scale=-DECAY).then_inc(s.decays, 1)
                n = 0
                for dst in (btok, ktok, vtok):
                    for g in range(2):
                        act.wait_ge(s.tok_mm, 6 * i + n + 1)
                        act.copy(dst[:, 4 * g:4 * g + 4, :].rearrange("p c t -> p (c t)"), bank[n % 4][:, :]
                                 ).then_inc(s.tok_ev, 1)
                        n += 1
                for l in range(1, NL):
                    for g in range(2):
                        act.wait_ge(s.x_mm, 10 * i + 2 * (l - 1) + g + 1)
                        act.copy(X[:, 4 * g:4 * g + 4, :].rearrange("p c t -> p (c t)"), X_ps[g][:, :]
                                 ).then_inc(s.x_ev, 1)
                for c in range(NCH):
                    act.wait_ge(s.r_mm, 8 * i + c + 1)
                    act.copy(Rc[:, :], R_ps).then_inc(s.r_ev, 1)
                    if c == 1:
                        act.wait_ge(s.stok_mm, i + 1)
                        act.copy(toks[:, :, :].rearrange("p n t -> p (n t)"), A[1][0:S2, 0:3 * P]).then_inc(s.stok_ev, 1)
                    if c == 2:
                        act.wait_ge(s.sx_mm, i + 1)
                        act.copy(Xs[:, :], A[0][0:S2, 256:320]).then_inc(s.sx_ev, 1)
                    if c == 4:
                        act.wait_ge(s.srt_mm, i + 1)
                        act.copy(RTs[:, :], B[0][:, 0:S2]).then_inc(s.srt_ev, 1)
                    if c == 5:
                        act.wait_ge(s.sr_mm, i + 1)
                        act.copy(Rs[:, :], A[1][0:S2, 384:512]).then_inc(s.sr_ev, 1)
                    if c == 6:
                        act.wait_ge(s.su_mm, i + 1)
                        act.copy(Us[:, :], A[0][0:S2, 384:512]).then_inc(s.su_ev, 1)
                act.wait_ge(s.sy_mm, i + 1)
                act.copy(ybuf[:, SEQ:T], B[0][:, 64:96]).then_inc(s.y_ev, 1)
                act.wait_ge(s.yc_mm, 8 * i + 8)
                act.copy(ybuf[:, 0:SEQ], y_ps).then_inc(s.y_ev, 1)
                act.wait_ge(s.yc, i + 1)
                act.activation(ksq[:, :], rk[:, :], ACT.Square).then_inc(s.ysq, 1)
                act.wait_ge(s.var_mm, i + 1)
                recip_root(act, halves(rn[:, :]), pB[:, :, 0:TH], 1.0, eps[:, 1:2], s.gln, s.grs, i + 1)

        @block.gpsimd
        def _(pool):
            for t in (aE, bE, kE, vE, SEs):
                pool.memset(t[:, :, :], 0.0).then_inc(s.zeroed, 1)
            pool.memset(vEs[:, :], 0.0).then_inc(s.zeroed, 1)
            pool.memset(arS[:, :], 0.0)
            pool.memset(bEs[:, :], 0.0)
            pool.memset(kEs[:, :], 0.0).then_inc(s.zeroed, 1)
            pool.wait_ge(s.const_in, 16 * len(names))
            pool.wait_ge(s.zeroed, 7)
            pool.sem_inc(s.vm_all, 1)
            with pool.Fori(0, KT) as i:
                pool.wait_ge(s.vm_all, i + 1)
                pool.wait_ge(s.k2, i + 1)
                pool.wait_ge(s.decays, 3 * i + 2)
                for hh in range(2):
                    rows = slice(64 * hh, 64 * hh + 64)
                    if hh:
                        pool.wait_ge(s.expand_pool, 4 * i + 2)
                    pool.tensor_tensor(kE[rows, :, rows], prompt(k2, hh), prompt(Wi, hh), ALU.mult
                                       ).then_inc(s.expand_pool, 1)
                    pool.wait_ge(s.expand_pool, 4 * i + 2 * hh + 1)
                    pool.tensor_tensor(kEs[rows, SMP * hh:SMP * hh + SMP], k2[rows, SEQ:T], Wi[rows, SEQ:T],
                                       ALU.mult).then_inc(s.expand_pool, 1)
                pool.wait_ge(s.expand_pool, 4 * i + 4)
                pool.wait_ge(s.mab, 2 * i + 2)
                for l in range(NL):
                    for g in range(2):
                        ins = pool.tensor_tensor(Mlev[l][:, 4 * g:4 * g + 4, :].rearrange("p c t -> p (c t)"),
                                                 Mab[:, 4 * g:4 * g + 4, :].rearrange("p c t -> p (c t)"),
                                                 lev[l][:, :], ALU.mult)
                    ins.then_inc(s.lev_r, 1)
                We = W[:, SEQ + DS - 1:T:DS].unsqueeze(2).broadcast_to([P, NB, HD])
                pool.tensor_tensor(sdec[:, :, :], Sc[:, :, :], We, ALU.mult).then_inc(s.sdec, 1)
                pool.wait_ge(s.sdec, i + 1)
                pool.wait_ge(s.stok_ev, i + 1)
                for hh in range(2):
                    rows = slice(SMP * hh, SMP * hh + SMP)
                    src = toks[rows, 0:1, 64 * hh:64 * hh + 64].broadcast_to([SMP, NB, HD])
                    if hh:
                        pool.wait_ge(s.vm, 2 * i + 1)
                    pool.tensor_tensor(Vm[rows, :, :], src, k.s_seq[rows, :].rearrange("p (b v) -> p b v", v=HD),
                                       ALU.mult).then_inc(s.vm, 1)
                pool.wait_ge(s.vm, 2 * i + 2)
                pool.sem_inc(s.vm_all, 1)

        @block.vector
        def _(dve):
            dve.wait_ge(s.const_in, 16 * len(names))
            dve.wait_ge(s.zeroed, 7)
            with dve.Fori(0, KT) as i:
                dve.wait_ge(s.loaded, (i + 1) * (16 * LOADS))
                dve.wait_ge(s.abs_r, 3 * i + 3)
                dve.tensor_scalar(halves(mn3[:, 0, :]), pA[:, :, 0:TH], col_of("w0"), 0.0, ALU.add, ALU.min
                                  ).then_inc(s.min3, 1)
                dve.tensor_scalar(halves(mn3[:, 1, :]), pB[:, :, 0:TH], col_of("a0"), 0.0, ALU.add, ALU.min
                                  ).then_inc(s.min3, 1)
                dve.tensor_scalar(mn3[:, 2, :], zt[:, :], 0.0, None, ALU.min).then_inc(s.min3, 1)
                dve.wait_ge(s.ln3, i + 1)
                dve.wait_ge(s.min3, 3 * i + 3)
                dve.tensor_tensor(mn3[:, :, :], mn3[:, :, :], e3[:, :, :], ALU.subtract).then_inc(s.ls3, 1)
                dve.wait_ge(s.ss_mm, i + 1)
                dve.tensor_scalar(halves(ssm[:, :]), pA[:, :, 0:TH], 1e-24, None, ALU.max).then_inc(s.ssm, 1)
                dve.wait_ge(s.sg3, i + 1)
                dve.tensor_tensor_scan(cs[:, :], k.reset[:, :], sg3[:, 0, :], 0.0, ALU.mult, ALU.add
                                       ).then_inc(s.scan, 1)
                dve.tensor_scalar(kf[:, :], sg3[:, 1, :], 1.0, col_of("k_a"), ALU.subtract, ALU.mult
                                  ).then_inc(s.kf, 1)
                dve.wait_ge(s.scan, i + 1)
                dve.tensor_tensor(csx[:, :], cs[:, :], sg3[:, 0, :], ALU.subtract).then_inc(s.csx, 1)
                dve.wait_ge(s.kf, i + 1)
                dve.scalar_tensor_tensor(k2[:, :], kf[:, :], 1.0, kt_[:, :], ALU.add, ALU.mult).then_inc(s.k2, 1)
                dve.wait_ge(s.k2, i + 1)
                dve.scalar_tensor_tensor(rk[:, :], rt[:, :], col_of("r_k"), k2[:, :], ALU.mult, ALU.mult
                                         ).then_inc(s.rk, 1)
                dve.wait_ge(s.rn, i + 1)
                dve.scalar_tensor_tensor(kkn[:, :], kt_[:, :], col_of("k_k"), rn[:, :], ALU.mult, ALU.mult
                                         ).then_inc(s.kkn, 1)
                dve.wait_ge(s.kkn, i + 1)
                dve.tensor_tensor(bb[:, :], kkn[:, :], sg3[:, 1, :], ALU.mult).then_inc(s.bb, 1)
                dve.tensor_tensor(zs[:, :], zt[:, :], sg3[:, 2, :], ALU.mult).then_inc(s.zs, 1)
                dve.wait_ge(s.decays, 3 * i + 3)
                dve.wait_ge(s.bb, i + 1)
                dve.tensor_tensor(rho[:, :], rt[:, :], W[:, :], ALU.mult).then_inc(s.expand, 1)
                dve.tensor_tensor(rhoS, rt[:, SEQ:T], W[:, SEQ:T], ALU.mult).then_inc(s.expand, 1)
                for hh in range(2):
                    rows = slice(64 * hh, 64 * hh + 64)
                    smp = slice(SMP * hh, SMP * hh + SMP)
                    dve.scalar_tensor_tensor(aE[rows, :, rows], prompt(kkn, hh), -1.0, prompt(Wp, hh),
                                             ALU.mult, ALU.mult).then_inc(s.expand, 1)
                    dve.tensor_tensor(bE[rows, :, rows], prompt(bb, hh), prompt(Wi, hh), ALU.mult
                                      ).then_inc(s.expand, 1)
                    dve.scalar_tensor_tensor(arS[rows, smp], kkn[rows, SEQ:T], -1.0, Wp[rows, SEQ:T],
                                             ALU.mult, ALU.mult).then_inc(s.expand, 1)
                    dve.tensor_tensor(bEs[rows, smp], bb[rows, SEQ:T], Wi[rows, SEQ:T], ALU.mult
                                      ).then_inc(s.expand, 1)
                dve.wait_ge(s.bonus_mm, i + 1)
                dve.tensor_tensor(halves(bv[:, :]), pB[:, :, 0:TH], halves(vt[:, :]), ALU.mult).then_inc(s.bv, 1)
                We4 = W[:, SEQ + DS - 1:T:DS].unsqueeze(1).unsqueeze(3).broadcast_to([P, 2, NB, DS])
                v4 = "p (h b j) -> p h b j"
                dve.wait_ge(s.expand, 10 * i + 10)
                dve.tensor_tensor(bds[:, :].rearrange(v4, h=2, b=NB), bEs[:, :].rearrange(v4, h=2, b=NB), We4,
                                  ALU.mult).then_inc(s.bds, 1)
                dve.wait_ge(s.expand_pool, 4 * i + 4)
                dve.tensor_tensor(kds[:, :].rearrange(v4, h=2, b=NB), kEs[:, :].rearrange(v4, h=2, b=NB), We4,
                                  ALU.mult).then_inc(s.kds, 1)

                def group(t, g):
                    return t[:, 4 * g:4 * g + 4, :].rearrange("p c t -> p (c t)")

                for g in range(2):
                    dve.wait_ge(s.mab_mm, 2 * i + g + 1)
                    dve.tensor_tensor(group(Mab, g), bank[g][:, :], k.strict[:, :], ALU.mult).then_inc(s.mab, 1)
                for g in range(2):
                    dve.wait_ge(s.mabn_mm, 2 * i + g + 1)
                    dve.tensor_tensor(group(Ti, g), bank[2 + g][:, :], k.lev1n[:, :], ALU.mult).then_inc(s.ti_lev, 1)
                for g in range(2):
                    dve.wait_ge(s.ti_lev, 2 * i + g + 1)
                    dve.tensor_tensor(group(Ti, g), group(Ti, g), k.eye4[:, :], ALU.add).then_inc(s.ti0, 1)
                for g in range(2):
                    dve.wait_ge(s.mak_mm, 2 * i + g + 1)
                    dve.tensor_tensor(group(Mak, g), A[g], k.strict[:, :], ALU.mult).then_inc(s.makd, 1)
                dve.wait_ge(s.mrb_mm, i + 1)
                dve.tensor_tensor(Mrb[:, :, :].rearrange("p c t -> p (c t)"), B[0], k.incl[:, :], ALU.mult
                                  ).then_inc(s.mrbd, 1)
                dve.wait_ge(s.mrk_mm, i + 1)
                dve.tensor_tensor(Mrk[:, :, :].rearrange("p c t -> p (c t)"), B[1], k.incl[:, :], ALU.mult
                                  ).then_inc(s.mrkd, 1)
                dve.wait_ge(s.lev_r, 6 * i + 1)
                dve.tensor_tensor(group(TiT, 0), group(Mlev[0], 0), k.eye4[:, :], ALU.add)
                dve.tensor_tensor(group(TiT, 1), group(Mlev[0], 1), k.eye4[:, :], ALU.add).then_inc(s.tit0, 1)
                dve.wait_ge(s.tit0, i + 1)
                for l in range(1, NL):
                    for g in range(2):
                        if l < NL - 1:
                            dve.wait_ge(s.y_mm, 8 * i + 2 * (l - 1) + g + 1)
                            if l > 1:
                                dve.wait_ge(s.ti_r, 8 * i + 2 * (l - 2) + g + 1)
                            dve.tensor_tensor(group(Ti, g), Y_ps[g][:, :], group(Ti, g), ALU.add).then_inc(s.ti_r, 1)
                        dve.wait_ge(s.yt_mm, 10 * i + 2 * (l - 1) + g + 1)
                        if l > 1:
                            dve.wait_ge(s.tit_r, 10 * i + 2 * (l - 2) + g + 1)
                        dve.tensor_tensor(group(TiT, g), YT_ps[g], group(TiT, g), ALU.add).then_inc(s.tit_r, 1)
                for c in range(NCH):
                    dve.wait_ge(s.u_mm, 8 * i + c + 1)
                    dve.tensor_copy(Uc[:, :], U_ps).then_inc(s.u_ev, 1)
                    if c == 0:
                        dve.wait_ge(s.sm_mm, i + 1)
                        dve.tensor_tensor(Ms[:, :, :].rearrange("p n t -> p (n t)"), A[0][0:S2, 0:192],
                                          k.s_mask[0:S2, :], ALU.mult).then_inc(s.sms, 1)
                        dve.tensor_tensor(Tis[:, :], A[0][0:S2, 192:256], k.s_lev1n[0:S2, :], ALU.mult
                                          ).then_inc(s.smt, 1)
                        dve.wait_ge(s.sms, i + 1)
                        dve.tensor_tensor(M1s[:, :], Ms[:, 0, 0:S2], k.s_lev1[0:S2, :], ALU.mult).then_inc(s.smd, 1)
                    if c == 1:
                        dve.tensor_tensor(M2s[:, :], Ms[:, 0, 0:S2], k.s_lev2[0:S2, :], ALU.mult).then_inc(s.smt0, 1)
                        dve.wait_ge(s.smd, i + 1)
                        dve.tensor_tensor(TiTs[:, :], M1s[:, :], k.s_eye[0:S2, :], ALU.add)
                        dve.wait_ge(s.smt, i + 1)
                        dve.tensor_tensor(Tis[:, :], Tis[:, :], k.s_eye[0:S2, :], ALU.add).then_inc(s.smt0, 1)
                    if c == 3:
                        dve.wait_ge(s.syt_mm, i + 1)
                        dve.wait_ge(s.smt0, 2 * i + 2)
                        dve.tensor_tensor(TiTs[:, :], A[0][0:S2, 320:384], TiTs[:, :], ALU.add).then_inc(s.stit, 1)
                    if c == 7:
                        dve.wait_ge(s.su_ev, i + 1)
                        for hh in range(2):
                            rows = slice(SMP * hh, SMP * hh + SMP)
                            src = Us[rows, 64 * hh:64 * hh + 64].unsqueeze(1).broadcast_to([SMP, NB, HD])
                            dve.tensor_tensor(Um[rows, :, :], src, k.s_seq[rows, :].rearrange(
                                "p (b v) -> p b v", v=HD), ALU.mult).then_inc(s.um, 1)
                    dve.wait_ge(s.s_mm, 8 * i + c + 1)
                    if c == NCH - 1:
                        dve.wait_ge(s.yc_mm, 8 * i + 8)
                    dve.tensor_scalar(SE[:, :], S_ps, W[:, c * C + C - 1:c * C + C], None, ALU.mult
                                      ).then_inc(s.s_ev, 1)
                dve.wait_ge(s.s_ev, 8 * i + 8)
                for hh in range(2):
                    rows = slice(64 * hh, 64 * hh + 64)
                    dve.tensor_copy(sfin[rows, :], SE[rows, rows]).then_inc(s.sfin, 1)
                dve.wait_ge(s.sd_mm, i + 1)
                dve.wait_ge(s.sdec, i + 1)
                dve.tensor_tensor(snew[:, :, :].rearrange("p b v -> p (b v)"), B[1],
                                  sdec[:, :, :].rearrange("p b v -> p (b v)"), ALU.add).then_inc(s.snew, 1)
                dve.wait_ge(s.mean_mm, i + 1)
                dve.tensor_tensor(halves(rk[:, :]), halves(ybuf[:, :]), pA[:, :, 0:TH], ALU.subtract).then_inc(s.yc, 1)
                dve.wait_ge(s.grs, i + 1)
                dve.wait_ge(s.yc, i + 1)
                dve.tensor_tensor(rk[:, :], rk[:, :], rn[:, :], ALU.mult).then_inc(s.yn, 1)
                dve.wait_ge(s.yn, i + 1)
                dve.tensor_scalar(rk[:, :], rk[:, :], col_of("ln_w"), col_of("ln_b"), ALU.mult, ALU.add
                                  ).then_inc(s.yw, 1)
                dve.wait_ge(s.yw, i + 1)
                dve.tensor_tensor(rk[:, :], rk[:, :], bv[:, :], ALU.add).then_inc(s.yb, 1)
                dve.wait_ge(s.yb, i + 1)
                dve.tensor_tensor(ybuf[:, :], rk[:, :], zs[:, :], ALU.mult).then_inc(s.yz, 1)


def hgrn(nc, keep, d):
    with ExitStack() as ctx:
        R = Region(nc, ctx, "e")
        sb, ps = R.sb, R.ps
        eps = keep.eps
        names = ["ident", "ones", "reset", "h_seq"] + [f"h_lev{m}" for m in HGRN_LEVELS]
        tables = {n: sb(f"k_{n}", [P, keep.col[n][1]]) for n in names}
        k = named(**tables)
        x_hi, x_lo = sb("x_hi", [P, KT, T], F32R), sb("x_lo", [P, KT, T], F32R)
        raw = [sb(f"raw{b}", [P, D]) for b in range(2)]
        w_hi = [sb(f"w_hi{b}", [P, D], F32R) for b in range(2)]
        w_lo = [sb(f"w_lo{b}", [P, D], F32R) for b in range(2)]
        lb, oml = sb("lb", [P, KT]), sb("oml", [P, KT])
        x3, e3, m3 = (sb(n, [P, 3, T]) for n in ("x3", "e3", "m3"))
        v, G, kg, qs, zs, fl, fb, Dm, qS, kS, o = (
            sb(n, [P, T]) for n in ("v", "G", "kg", "qs", "zs", "fl", "fb", "Dm", "qS", "kS", "o"))
        hx = [fl, fb]
        ex, Kx, Qx = ([sb(f"{n}{b}", [P, T]) for b in range(2)] for n in ("ex", "Kx", "Qx"))
        eg, eblk = sb("eg", [P, NCH + NB]), sb("eblk", [P, 4])
        A, At = sb("A", [P, SEQ]), [sb(f"At{b}", [P, SEQ]) for b in range(2)]
        As, Ast = sb("As", [SMP, SMP]), [sb(f"Ast{b}", [SMP, SMP]) for b in range(2)]
        vtok, ktok = sb("vtok", [P, 5, P]), sb("ktok", [P, 5, P])
        S = sb("S", [P, P])
        Ss, Sd = sb("Ss", [P, NB, P]), sb("Sd", [P, NB, P])
        Vm = sb("Vm", [SMP, NB, P])
        pair = [ps(f"pair{b}", [P, 2, 512]) for b in range(2)]
        bank = [ps(f"bank{n}", [P, 512]) for n in range(4)]
        HL = len(HGRN_LEVELS)
        mask = [tables[f"h_lev{m}"] for m in HGRN_LEVELS]
        s = R.sems("const_in hx_in0 hx_in1 hx_hi hx_lo zeroed lb_a lb_b "
                   "raw_in0 raw_in1 raw_hi0 raw_hi1 raw_lo0 raw_lo1 tile_ready0 tile_ready1 evac0 evac1 "
                   "states_in s_out sn_out yz_out as_a added_s "
                   "abs3 exp3 ln3 min3 mneg ls3 lneg sg3 kraw kg fl fa fb_ la lc g G qs zs "
                   "dk dke qe kS qS eg eblk scaled "
                   "dm ex1 ex2 kx qx lev_mm at added as_mm as_r a64 "
                   "vt_mm vtok kt_mm ktok o_mm s_mm s_r so_mm sd vm sn_mm sn "
                   "o_ev osq ss_mm ln rs on yz")
        raw_in, raw_hi, raw_lo = [s.raw_in0, s.raw_in1], [s.raw_hi0, s.raw_hi1], [s.raw_lo0, s.raw_lo1]
        hx_in = [s.hx_in0, s.hx_in1]
        tile_ready, evac = [s.tile_ready0, s.tile_ready1], [s.evac0, s.evac1]
        block = ctx.enter_context(nc.Block())
        NLV = HL + 2

        def width(m):
            return T if m < DS else SEQ

        def parts(t, m):
            return t[:, 0:width(m)].rearrange("p (b h m) -> p b h m", h=2, m=m)

        def by4(t):
            return t[:, :].rearrange("p (c t) -> p c t", t=P)

        def over4(t):
            return t[:, :].unsqueeze(1).broadcast_to([P, 4, P])

        def blk(t, c):
            return t[:, c * P:(c + 1) * P]

        @block.sync
        def _(sp):
            for n in names:
                sp.dma_start(tables[n][:, :], keep.const(n)).then_inc(s.const_in, 16)
            for kt in range(KT):
                if kt == 2:
                    for b in range(2):
                        sp.dma_start(raw[b][:, :], d.hgrn_in[b]).then_inc(raw_in[b], 16)
                if kt >= 2:
                    sp.wait_ge(s.hx_lo, kt - 1)
                sp.dma_start(hx[kt % 2][:, :], d.h1[kt]).then_inc(hx_in[kt % 2], 16)

            def weights(pr):
                for b in range(2):
                    sp.wait_ge(raw_hi[b], pr + 1)
                    sp.wait_ge(raw_lo[b], pr + 1)
                    sp.dma_start(raw[b][:, :], dram_tile(d.hgrn_in, 2 * pr + b)).then_inc(raw_in[b], 16)

            def states(e):
                sp.dma_start(Ss[:, :, :], d.hgrn_s[bass.ds(e, 1), :, :, :].rearrange("a p b v -> p (a b) v")
                             ).then_inc(s.states_in, 16)

            def stores(e):
                sp.wait_ge(s.s_r, 4 * e + 8)
                sp.dma_start(dram_tile(d.hgrn_p, e), S[:, :]).then_inc(s.s_out, 16)
                sp.wait_ge(s.sn, 2 * e + 2)
                sp.dma_start(d.hgrn_so[bass.ds(e, 1), :, :, :].rearrange("a p b v -> p (a b) v"), Sd[:, :, :]
                             ).then_inc(s.sn_out, 16)
                sp.wait_ge(s.yz, e + 1)
                sp.dma_start(dram_tile(d.yz, e), o[:, :]).then_inc(s.yz_out, 16)

            weights(1)
            states(0)
            weights(2)
            weights(3)
            with sp.Fori(1, KT - 1) as e:
                weights(2 * e + 2)
                sp.wait_ge(s.sd, e)
                sp.wait_ge(s.so_mm, e)
                states(e)
                stores(e - 1)
                weights(2 * e + 3)
            sp.wait_ge(s.sd, KT - 1)
            sp.wait_ge(s.so_mm, KT - 1)
            states(KT - 1)
            stores(KT - 2)
            stores(KT - 1)
            for out in (s.s_out, s.sn_out, s.yz_out):
                sp.wait_ge(out, 16 * (KT + 1))

        @block.tensor
        def _(pe):
            for b in range(2):
                pe.sem_inc(tile_ready[b], 1)
            pe.wait_ge(s.const_in, 16 * len(names))
            pe.wait_ge(s.hx_lo, KT)

            def dense(b, j, hooks):
                pe.wait_ge(raw_hi[b], j + 2)
                pe.wait_ge(raw_lo[b], j + 2)
                pe.wait_ge(evac[b], j + 1)
                for kt in range(KT):
                    hi, lo = w_hi[b][:, kt * P:(kt + 1) * P], w_lo[b][:, kt * P:(kt + 1) * P]
                    for n, (w, x) in enumerate(((hi, x_hi), (hi, x_lo), (lo, x_hi))):
                        for a in range(2):
                            mm = pe.matmul(pair[b][:, a, 0:TH], w, x[:, kt, a * TH:(a + 1) * TH],
                                           start=(kt == 0 and n == 0), stop=(kt == KT - 1 and n == 2))
                    if kt == KT - 1:
                        mm.then_inc(tile_ready[b], 1)
                    if kt % 4 == 3 and hooks and hooks[kt // 4]:
                        hooks[kt // 4]()

            def v_by_token(e):
                pe.wait_ge(evac[1], 2 * e + 3)
                pe.wait_ge(s.o_ev, 2 * e + 2)
                pe.wait_ge(s.s_r, 4 * e + 4)
                for c in range(4):
                    pe.transpose(blk(bank[2], c), blk(v, c), k.ident[:, :])
                pe.transpose(bank[3][0:SMP, P:2 * P], v[:, SEQ:T], k.ident[:, :]).then_inc(s.vt_mm, 1)

            def k_by_token(e):
                pe.wait_ge(s.scaled, 2 * e + 2)
                pe.wait_ge(s.vtok, 2 * e + 2)
                for c in range(4):
                    pe.transpose(blk(bank[2], c), blk(kS, c), k.ident[:, :])
                pe.transpose(bank[3][0:SMP, 2 * P:3 * P], kS[:, SEQ:T], k.ident[:, :]).then_inc(s.kt_mm, 1)

            def level_mm(e, n):
                bk = bank[n % 2]
                if n == 0:
                    pe.wait_ge(s.kg, e + 1)
                    pe.wait_ge(s.qs, e + 1)
                    pe.wait_ge(s.rs, e + 1)
                    K, Q = kg, qs
                elif n == 1:
                    pe.wait_ge(s.kS, e + 1)
                    pe.wait_ge(s.qS, e + 1)
                    for c in range(4):
                        mm = pe.matmul(bk[0:64, c * 64:(c + 1) * 64], kS[:, c * P:c * P + 64],
                                       qS[:, c * P + 64:(c + 1) * P], start=True, stop=True)
                    mm.then_inc(s.lev_mm, 1)
                    return
                else:
                    K, Q = Kx[n % 2], Qx[n % 2]
                    pe.wait_ge(s.kx, HL * e + n - 1)
                    pe.wait_ge(s.qx, HL * e + n - 1)
                    pe.wait_ge(s.at, NLV * e + n - 1)
                for c in range(4):
                    mm = pe.matmul(blk(bk, c), blk(K, c), blk(Q, c), start=True, stop=True)
                mm.then_inc(s.lev_mm, 1)
                if n in (0, 2, 3):
                    if n == 0:
                        pe.wait_ge(s.vtok, 2 * e + 2)
                    else:
                        pe.wait_ge(s.as_r, 3 * e + (n - 1))
                    pe.matmul(bank[3][0:SMP, 0:SMP], K[:, SEQ:T], Q[:, SEQ:T], start=True, stop=True
                              ).then_inc(s.as_mm, 1)

            def chain(e, c):
                if c == 0:
                    pe.wait_ge(s.added, HL * e + HL)
                    pe.wait_ge(s.ktok, 2 * e + 2)
                    pe.wait_ge(s.as_r, 3 * e + 3)
                pe.matmul(blk(bank[2], c), vtok[:, c, :], blk(A, c), start=True, stop=(c == 0))
                if c:
                    pe.wait_ge(s.s_r, 4 * e + c + 4)
                    mm = pe.matmul(blk(bank[2], c), S[:, :], blk(qS, c), start=False, stop=True)
                pe.matmul(bank[3][:, 3 * P:4 * P], ktok[:, c, :], vtok[:, c, :], start=True, stop=True
                          ).then_inc(s.s_mm, 1)

            def sample_out(e):
                pe.wait_ge(s.states_in, 16 * e + 16)
                pe.wait_ge(s.as_r, 3 * e + 4 - 1)
                pe.wait_ge(s.at, NLV * e + NLV)
                for b in range(NB):
                    pe.matmul(bank[1][:, DS * b:DS * b + DS], Ss[:, b, :], qS[:, SEQ + DS * b:SEQ + DS * b + DS],
                              start=(b == 0), stop=False, skip_group_check=True)
                pe.wait_ge(s.added_s, e + 1)
                pe.matmul(bank[1][:, 0:SMP], vtok[0:SMP, 4, :], As[:, :], start=False, stop=True,
                          skip_group_check=True).then_inc(s.so_mm, 1)

            def sample_state(e, hb):
                pe.wait_ge(s.vm, e + 1)
                if hb:
                    pe.wait_ge(s.sn, 2 * e + 1)
                pe.matmul(bank[0][:, :], ktok[0:SMP, 4, :],
                          Vm[:, 4 * hb:4 * hb + 4, :].rearrange("p b v -> p (b v)"), start=True, stop=True
                          ).then_inc(s.sn_mm, 1)

            def norm(e):
                pe.wait_ge(s.osq, e + 1)
                pe.wait_ge(s.sn, 2 * e + 2)
                for a in range(2):
                    mm = pe.matmul(bank[a][:, 0:TH], k.ones[:, :], Dm[:, a * TH:(a + 1) * TH], start=True, stop=True)
                mm.then_inc(s.ss_mm, 1)

            for b in range(2):
                dense(b, 0, None)
            for b in range(2):
                dense(b, 1, None)

            def steps(e):
                L = lambda n: (lambda: level_mm(e, n))
                return [[None, lambda: v_by_token(e), None, L(0)],
                        [L(1), lambda: k_by_token(e), L(2), L(3)],
                        [L(4), L(5), L(6), L(7)],
                        [lambda: chain(e, 0), lambda: (chain(e, 1), sample_out(e), sample_state(e, 0)),
                         lambda: (chain(e, 2), sample_state(e, 1)), lambda: chain(e, 3)]]

            with pe.Fori(0, KT - 1) as e:
                st = steps(e)
                for jj in range(2):
                    for b in range(2):
                        dense(b, 2 * e + (2 + jj), st[2 * jj + b])
                norm(e)
            for four in steps(KT - 1):
                for step in four:
                    if step:
                        step()
            norm(KT - 1)

        @block.scalar
        def _(act):
            for b in range(2):
                act.sem_inc(raw_hi[b], 1)
                act.sem_inc(evac[b], 1)
            act.sem_inc(s.o_ev, 2)
            act.sem_inc(s.rs, 1)

            def split_hi(b, j):
                act.wait_ge(raw_in[b], 16 * (j + 1))
                act.wait_ge(tile_ready[b], j + 1)
                act.copy(w_hi[b][:, :], raw[b][:, :]).then_inc(raw_hi[b], 1)

            def evacuate(b, j, dst):
                act.wait_ge(tile_ready[b], j + 2)
                act.copy(halves(dst), pair[b][:, :, 0:TH]).then_inc(evac[b], 1)

            for kt in range(KT):
                act.wait_ge(hx_in[kt % 2], 16 * (kt // 2 + 1))
                act.copy(x_hi[:, kt, :], hx[kt % 2][:, :]).then_inc(s.hx_hi, 1)
            act.wait_ge(s.lb_a, 1)
            act.activation(oml[:, :], oml[:, :], ACT.Exp).then_inc(s.lb_b, 1)
            for b in range(2):
                split_hi(b, 0)
            for b in range(2):
                evacuate(b, 0, x3[:, b, :])
                split_hi(b, 1)
            evacuate(0, 1, x3[:, 2, :])
            split_hi(0, 2)
            evacuate(1, 1, v[:, :])
            split_hi(1, 2)

            def gates(e):
                act.wait_ge(evac[0], 2 * e + 3)
                act.wait_ge(evac[1], 2 * e + 3)
                act.wait_ge(s.rs, e + 1)
                act.wait_ge(s.on, e + 1)
                act.activation(e3[:, :, :], x3[:, :, :], ACT.Abs).then_inc(s.abs3, 1)
                act.wait_ge(s.abs3, e + 1)
                act.activation(e3[:, :, :], e3[:, :, :], ACT.Exp, scale=-1.0).then_inc(s.exp3, 1)
                act.wait_ge(s.exp3, e + 1)
                act.activation(e3[:, :, :], e3[:, :, :], ACT.Ln, bias=1.0).then_inc(s.ln3, 1)
                act.wait_ge(s.ls3, e + 1)
                act.activation(m3[:, :, :], m3[:, :, :], ACT.Exp).then_inc(s.sg3, 1)
                act.wait_ge(s.lneg, e + 1)
                act.activation(kg[:, :], kg[:, :], ACT.Exp).then_inc(s.kraw, 1)
                act.wait_ge(s.fa, e + 1)
                act.activation(fl[:, :], fl[:, :], ACT.Ln).then_inc(s.la, 1)
                act.wait_ge(s.fb_, e + 1)
                act.activation(fb[:, :], fb[:, :], ACT.Ln, scale=1.0 / LN_SPLIT).then_inc(s.lc, 1)

            def v_copy(e):
                act.wait_ge(s.vt_mm, e + 1)
                act.copy(vtok[:, 0:4, :].rearrange("p c t -> p (c t)"), bank[2][:, :]).then_inc(s.vtok, 1)
                act.copy(vtok[0:SMP, 4, :], bank[3][0:SMP, P:2 * P]).then_inc(s.vtok, 1)

            def k_copy(e):
                act.wait_ge(s.kt_mm, e + 1)
                act.copy(ktok[:, 0:4, :].rearrange("p c t -> p (c t)"), bank[2][:, :]).then_inc(s.ktok, 1)
                act.wait_ge(s.as_r, 3 * e + 1)
                act.copy(ktok[0:SMP, 4, :], bank[3][0:SMP, 2 * P:3 * P]).then_inc(s.ktok, 1)

            def decays(e):
                act.wait_ge(s.G, e + 1)
                act.activation(e3[:, 0, :], G[:, :], ACT.Exp).then_inc(s.qe, 1)
                act.wait_ge(s.dk, 2 * e + 2)
                act.activation(e3[:, 1, :], e3[:, 1, :], ACT.Exp).then_inc(s.dke, 1)
                act.activation(eg[:, 0:NCH], G[:, C - 1:SEQ:C], ACT.Exp).then_inc(s.eg, 1)
                act.activation(eg[:, NCH:], G[:, SEQ + DS - 1:T:DS], ACT.Exp).then_inc(s.eg, 1)

            def level_exp(e, l):
                m = HGRN_LEVELS[l]
                act.wait_ge(s.dm, HL * e + l + 1)
                if l >= 2:
                    act.wait_ge(s.qx, HL * e + l - 1)
                act.activation(parts(ex[l % 2], m)[:, :, 0, :], parts(Dm, m)[:, :, 0, :], ACT.Exp, scale=-1.0
                               ).then_inc(s.ex1, 1)
                act.activation(parts(ex[l % 2], m)[:, :, 1, :], parts(Dm, m)[:, :, 1, :], ACT.Exp
                               ).then_inc(s.ex2, 1)

            def tail(e):
                act.wait_ge(s.so_mm, e + 1)
                act.wait_ge(s.yz_out, 16 * e + 16)
                act.copy(o[:, SEQ:T], bank[1][:, 0:SMP]).then_inc(s.o_ev, 1)
                act.wait_ge(s.s_mm, 4 * e + 4)
                act.copy(o[:, 0:SEQ], bank[2][:, :]).then_inc(s.o_ev, 1)
                act.wait_ge(s.o_ev, 2 * e + 4)
                act.activation(Dm[:, :], o[:, :], ACT.Square).then_inc(s.osq, 1)
                act.wait_ge(s.ss_mm, e + 1)
                for a in range(2):
                    act.activation(e3[:, 2, a * TH:(a + 1) * TH], bank[a][:, 0:TH], ACT.Ln, scale=1.0 / P,
                                   bias=eps[:, 0:1]).then_inc(s.ln, 1)
                act.wait_ge(s.ln, 2 * e + 2)
                act.activation(e3[:, 2, :], e3[:, 2, :], ACT.Exp, scale=-0.5).then_inc(s.rs, 1)

            def body(e, dense_too):
                def tile(jj, b, dst):
                    if dense_too:
                        evacuate(b, 2 * e + (2 + jj), dst)
                        if dense_too == "last" and jj:
                            return
                        split_hi(b, 2 * e + (3 + jj))
                gates(e)
                v_copy(e)
                if dense_too:
                    act.wait_ge(s.zs, e + 1)
                    act.wait_ge(s.mneg, e + 1)
                tile(0, 0, x3[:, 0, :])
                decays(e)
                k_copy(e)
                level_exp(e, 0)
                level_exp(e, 1)
                tile(0, 1, x3[:, 1, :])
                for l in range(2, HL):
                    level_exp(e, l)
                tile(1, 0, x3[:, 2, :])
                tile(1, 1, v[:, :])
                tail(e)

            with act.Fori(0, KT - 2) as e:
                body(e, "more")
            body(KT - 2, "last")
            body(KT - 1, "")

        @block.gpsimd
        def _(pool):
            for t in (*Kx, *Qx):
                pool.memset(t[:, :], 0.0).then_inc(s.zeroed, 1)
            pool.wait_ge(s.const_in, 16 * len(names))
            pool.wait_ge(s.zeroed, 4)
            with pool.Fori(0, KT) as e:
                pool.wait_ge(s.eg, 2 * e + 2)
                pool.wait_ge(s.states_in, 16 * e + 16)
                pool.wait_ge(s.sn_out, 16 * e + 16)
                pool.tensor_tensor(Sd[:, :, :], Ss[:, :, :], eg[:, NCH:].unsqueeze(2).broadcast_to([P, NB, P]),
                                   ALU.mult).then_inc(s.sd, 1)
                pool.wait_ge(s.vtok, 2 * e + 2)
                pool.wait_ge(s.sd, e + 1)
                pool.tensor_tensor(Vm[:, :, :], vtok[0:SMP, 4:5, :].broadcast_to([SMP, NB, P]),
                                   k.h_seq[0:SMP, :].unsqueeze(2).broadcast_to([SMP, NB, P]), ALU.mult).then_inc(s.vm, 1)
                pool.wait_ge(s.vm, e + 1)
                pool.wait_ge(s.a64, e + 1)
                for n in range(HL):
                    pool.wait_ge(s.at, NLV * e + n + 3)
                    pool.tensor_tensor(A[:, :], A[:, :], At[n % 2][:, :], ALU.add).then_inc(s.added, 1)
                    pool.wait_ge(s.added, HL * e + n + 1)

        @block.vector
        def _(dve):
            for b in range(2):
                dve.sem_inc(raw_lo[b], 1)
            dve.sem_inc(s.sn_out, 16)
            dve.sem_inc(s.yz_out, 16)
            dve.sem_inc(s.on, 1)
            dve.sem_inc(s.s_r, 4)
            dve.wait_ge(s.const_in, 16 * len(names))

            def split_lo(b, j):
                dve.wait_ge(raw_hi[b], j + 2)
                dve.wait_ge(tile_ready[b], j + 1)
                dve.tensor_tensor(w_lo[b][:, :], raw[b][:, :], w_hi[b][:, :].bitcast(F32),
                                  ALU.subtract).then_inc(raw_lo[b], 1)

            logits = keep.params[:, :, PAR.index("lb")]
            dve.tensor_tensor(oml[:, :], logits, logits, ALU.subtract).then_inc(s.lb_a, 1)
            for kt in range(KT):
                dve.wait_ge(s.hx_hi, kt + 1)
                dve.tensor_tensor(x_lo[:, kt, :], hx[kt % 2][:, :], x_hi[:, kt, :].bitcast(F32),
                                  ALU.subtract).then_inc(s.hx_lo, 1)
            dve.wait_ge(s.lb_b, 1)
            dve.reciprocal(lb[:, :], oml[:, :]).then_inc(s.lb_a, 1)
            dve.wait_ge(s.lb_a, 2)
            dve.tensor_tensor(oml[:, :], oml[:, :], lb[:, :], ALU.mult).then_inc(s.lb_a, 1)
            dve.wait_ge(s.lb_a, 3)
            dve.tensor_tensor(lb[:, :], oml[:, :], oml[:, :], ALU.subtract).then_inc(s.lb_a, 1)
            dve.wait_ge(s.lb_a, 4)
            dve.tensor_scalar(oml[:, :], lb[:, :], -1.0, 1.0, ALU.mult, ALU.add).then_inc(s.lb_a, 1)
            dve.wait_ge(s.lb_a, 5)
            for j in range(2):
                for b in range(2):
                    split_lo(b, j)
            for b in range(2):
                split_lo(b, 2)
            dve.wait_ge(s.zeroed, 4)

            def gates(e):
                lb_e, oml_e = (t[:, bass.ds(e, 1)] for t in (lb, oml))
                dve.wait_ge(evac[0], 2 * e + 3)
                dve.wait_ge(evac[1], 2 * e + 3)
                dve.tensor_scalar(m3[:, :, :], x3[:, :, :], 0.0, None, ALU.min).then_inc(s.min3, 1)
                dve.tensor_scalar(kg[:, :], x3[:, 0, :], -1.0, 0.0, ALU.mult, ALU.min).then_inc(s.mneg, 1)
                dve.wait_ge(s.min3, e + 1)
                dve.wait_ge(s.ln3, e + 1)
                dve.tensor_tensor(m3[:, :, :], m3[:, :, :], e3[:, :, :], ALU.subtract).then_inc(s.ls3, 1)
                dve.wait_ge(s.mneg, e + 1)
                dve.tensor_tensor(kg[:, :], kg[:, :], e3[:, 0, :], ALU.subtract).then_inc(s.lneg, 1)
                dve.wait_ge(s.sg3, e + 1)
                dve.tensor_scalar(Dm[:, :], m3[:, 0, :], oml_e, lb_e, ALU.mult, ALU.add).then_inc(s.fl, 1)
                dve.wait_ge(s.fl, e + 1)
                dve.tensor_scalar(fl[:, :], Dm[:, :], LN_SPLIT, None, ALU.max).then_inc(s.fa, 1)
                dve.tensor_scalar(fb[:, :], Dm[:, :], LN_SPLIT, GATE_FLOOR, ALU.min, ALU.max).then_inc(s.fb_, 1)
                dve.scalar_tensor_tensor(qs[:, :], x3[:, 1, :], float(P) ** -0.5, m3[:, 1, :], ALU.mult, ALU.mult
                                         ).then_inc(s.qs, 1)
                dve.tensor_tensor(zs[:, :], x3[:, 2, :], m3[:, 2, :], ALU.mult).then_inc(s.zs, 1)
                dve.wait_ge(s.kraw, e + 1)
                dve.tensor_scalar(kg[:, :], kg[:, :], oml_e, None, ALU.mult).then_inc(s.kg, 1)
                dve.wait_ge(s.la, e + 1)
                dve.wait_ge(s.lc, e + 1)
                dve.tensor_tensor(fl[:, :], fl[:, :], fb[:, :], ALU.add).then_inc(s.g, 1)
                dve.wait_ge(s.g, e + 1)
                dve.tensor_tensor_scan(G[:, :], k.reset[:, :], fl[:, :], 0.0, ALU.mult, ALU.add).then_inc(s.G, 1)
                dve.wait_ge(s.G, e + 1)
                for t0, t1, n in ((0, SEQ, C), (SEQ, T, DS)):
                    g3 = G[:, t0:t1].rearrange("p (c t) -> p c t", t=n)
                    dve.tensor_tensor(e3[:, 1, t0:t1].rearrange("p (c t) -> p c t", t=n),
                                      g3[:, :, n - 1:n].broadcast_to([P, (t1 - t0) // n, n]), g3,
                                      ALU.subtract).then_inc(s.dk, 1)

            def level_dm(e, l):
                m = HGRN_LEVELS[l]
                g3 = G[:, 0:width(m)].rearrange("p (b t) -> p b t", t=2 * m)
                if l:
                    dve.wait_ge(s.ex2, HL * e + l)
                dve.tensor_tensor(Dm[:, 0:width(m)].rearrange("p (b t) -> p b t", t=2 * m), g3,
                                  g3[:, :, m - 1:m].broadcast_to([P, width(m) // (2 * m), 2 * m]),
                                  ALU.subtract).then_inc(s.dm, 1)

            def level_kq(e, l):
                m = HGRN_LEVELS[l]
                dve.wait_ge(s.ex2, HL * e + l + 1)
                if l >= 2:
                    dve.wait_ge(s.lev_mm, NLV * e + l + 1)
                dve.tensor_tensor(parts(Kx[l % 2], m)[:, :, 0, :], parts(kg, m)[:, :, 0, :],
                                  parts(ex[l % 2], m)[:, :, 0, :], ALU.mult).then_inc(s.kx, 1)
                dve.tensor_tensor(parts(Qx[l % 2], m)[:, :, 1, :], parts(qs, m)[:, :, 1, :],
                                  parts(ex[l % 2], m)[:, :, 1, :], ALU.mult).then_inc(s.qx, 1)

            def take(e, n):
                dve.wait_ge(s.lev_mm, NLV * e + n + 1)
                if n == 0:
                    dve.tensor_tensor(by4(A), by4(bank[0]), over4(k.ident), ALU.mult).then_inc(s.at, 1)
                elif n == 1:
                    dve.wait_ge(s.at, NLV * e + 1)
                    dve.tensor_copy(A[0:64, :].rearrange("p (c t) -> p c t", t=P)[:, :, 64:P],
                                    bank[1][0:64, 0:256].rearrange("p (c t) -> p c t", t=64)).then_inc(s.at, 1)
                    dve.wait_ge(s.at, NLV * e + 2)
                    dve.sem_inc(s.a64, 1)
                else:
                    if n >= 4:
                        dve.wait_ge(s.added, HL * e + n - 3)
                    dve.tensor_tensor(by4(At[n % 2]), by4(bank[n % 2]), over4(mask[n - 2]), ALU.mult
                                      ).then_inc(s.at, 1)
                if n == 0:
                    dve.wait_ge(s.as_mm, 3 * e + 1)
                    dve.tensor_tensor(As[:, :], bank[3][0:SMP, 0:SMP], k.ident[0:SMP, 0:SMP], ALU.mult
                                      ).then_inc(s.as_r, 1)
                if n in (2, 3):
                    dve.wait_ge(s.as_mm, 3 * e + n)
                    dve.tensor_tensor(Ast[n % 2][:, :], bank[3][0:SMP, 0:SMP], mask[n - 2][0:SMP, 0:SMP], ALU.mult
                                      ).then_inc(s.as_r, 1)

            def body(e, dense_too):
                def split(b, jj):
                    if dense_too and not (dense_too == "last" and jj):
                        split_lo(b, 2 * e + (3 + jj))
                gates(e)
                take(e, 0)
                split(0, 0)
                dve.wait_ge(s.qe, e + 1)
                dve.tensor_tensor(qS[:, :], qs[:, :], e3[:, 0, :], ALU.mult).then_inc(s.qS, 1)
                dve.wait_ge(s.dke, e + 1)
                dve.tensor_tensor(kS[:, :], kg[:, :], e3[:, 1, :], ALU.mult).then_inc(s.kS, 1)
                take(e, 1)
                dve.wait_ge(s.eg, 2 * e + 2)
                q4 = qS[:, 0:SEQ].rearrange("p (c h t) -> p c h t", h=2, t=C)
                k4 = kS[:, 0:SEQ].rearrange("p (c h t) -> p c h t", h=2, t=C)
                dve.tensor_tensor(q4[:, :, 1, :], q4[:, :, 1, :],
                                  eg[:, 0:NCH:2].unsqueeze(2).broadcast_to([P, 4, C]), ALU.mult).then_inc(s.scaled, 1)
                dve.tensor_tensor(k4[:, :, 0, :], k4[:, :, 0, :],
                                  eg[:, 1:NCH:2].unsqueeze(2).broadcast_to([P, 4, C]), ALU.mult).then_inc(s.scaled, 1)
                dve.tensor_tensor(eblk[:, :], eg[:, 0:NCH:2], eg[:, 1:NCH:2], ALU.mult).then_inc(s.eblk, 1)
                level_dm(e, 0)
                level_kq(e, 0)
                level_dm(e, 1)
                split(1, 0)
                level_kq(e, 1)
                for l in range(2, HL + 2):
                    if l < HL:
                        level_dm(e, l)
                    take(e, l)
                    if l == 3:
                        dve.wait_ge(s.as_r, 3 * e + 3)
                        dve.tensor_tensor(As[:, :], As[:, :], Ast[0][:, :], ALU.add).then_inc(s.as_a, 1)
                        dve.wait_ge(s.as_a, e + 1)
                        dve.tensor_tensor(As[:, :], As[:, :], Ast[1][:, :], ALU.add).then_inc(s.added_s, 1)
                    if l < HL:
                        level_kq(e, l)
                    if l == 5:
                        split(0, 1)
                dve.wait_ge(s.s_out, 16 * e + 16)
                for c in range(4):
                    dve.wait_ge(s.s_mm, 4 * e + c + 1)
                    if c == 0:
                        dve.tensor_copy(S[:, :], bank[3][:, 3 * P:4 * P]).then_inc(s.s_r, 1)
                    else:
                        dve.wait_ge(s.s_r, 4 * e + c + 4)
                        dve.scalar_tensor_tensor(S[:, :], S[:, :], eblk[:, c:c + 1], bank[3][:, 3 * P:4 * P],
                                                 ALU.mult, ALU.add).then_inc(s.s_r, 1)
                    if c in (1, 2):
                        hb = c - 1
                        half_s = Sd[:, 4 * hb:4 * hb + 4, :].rearrange("p b v -> p (b v)")
                        dve.wait_ge(s.sn_mm, 2 * e + hb + 1)
                        dve.wait_ge(s.sd, e + 1)
                        dve.tensor_tensor(half_s, bank[0][:, :], half_s, ALU.add).then_inc(s.sn, 1)
                split(1, 1)
                dve.wait_ge(s.rs, e + 2)
                dve.scalar_tensor_tensor(o[:, :], o[:, :], par(keep.params, "norm_w", 0), e3[:, 2, :],
                                         ALU.mult, ALU.mult).then_inc(s.on, 1)
                dve.wait_ge(s.on, e + 2)
                dve.tensor_tensor(o[:, :], o[:, :], zs[:, :], ALU.mult).then_inc(s.yz, 1)

            dve.sem_inc(s.s_out, 16)
            with dve.Fori(0, KT - 2) as e:
                body(e, "more")
            body(KT - 2, "last")
            body(KT - 1, "")


def constants():
    i = np.arange(P)
    hs, ts = i // C, i % C
    same = hs[:, None] == hs[None, :]
    t = {}
    t["ones"] = np.ones((P, P))
    t["eps"] = np.tile(np.array([NORM_EPS, GN_EPS, 10 * np.log(2.0), 0.0]), (P, 1))
    t["ident"] = np.eye(P)
    t["bones"] = same * 1.0
    t["bmean"] = same / HD

    def level_t(tok, ok, m):
        a, b = tok[:, None], tok[None, :]
        return ok * (a // (2 * m) == b // (2 * m)) * (a % (2 * m) < m) * (b % (2 * m) >= m)

    t["strict"] = np.tile(same * (ts[:, None] < ts[None, :]), (1, 4))
    for m in RWKV_LEVELS:
        t[f"lev{m}"] = np.tile(level_t(ts, same, m), (1, 4))
    t["lev1n"] = np.tile(level_t(ts, same, 1).T, (1, 4))
    t["eye4"] = np.tile(np.eye(P), (1, 4))
    t["incl"] = np.tile(ts[:, None] <= np.arange(C)[None, :], (1, NCH))
    j = np.arange(2 * SMP)
    hh, tt = j // SMP, j % SMP
    samev = (hh[:, None] == hh[None, :]) & (tt[:, None] // DS == tt[None, :] // DS)
    pad = lambda a: np.concatenate([a, np.zeros((P - a.shape[0], a.shape[1]))])
    st = samev * (tt[:, None] < tt[None, :])
    u = np.arange(SMP)
    inc = (tt[:, None] // DS == u[None, :] // DS) & (tt[:, None] <= u[None, :])
    t["s_mask"] = pad(np.tile(np.concatenate([st, inc], 1), (1, 2)))
    t["s_lev1"] = pad(level_t(tt, samev, 1) * 1.0)
    t["s_lev2"] = pad(level_t(tt, samev, 2) * 1.0)
    t["s_lev1n"] = pad(level_t(tt, samev, 1).T * 1.0)
    t["s_eye"] = pad(np.eye(2 * SMP))
    t["s_seq"] = pad(np.repeat((tt[:, None] // DS == np.arange(NB)[None, :]) * 1.0, HD, 1))
    reset = np.ones(T)
    reset[0:SEQ:C] = 0
    reset[SEQ:T:DS] = 0
    t["reset"] = np.tile(reset, (P, 1))
    for m in HGRN_LEVELS:
        t[f"h_lev{m}"] = level_t(i, 1, m) * 1.0
    t["h_seq"] = pad((u[:, None] // DS == np.arange(NB)[None, :]) * 1.0)
    return t


def const_table():
    t, col, at, parts = constants(), {}, 0, []
    for n, a in t.items():
        col[n] = (at, a.shape[1])
        at += a.shape[1]
        parts.append(np.asarray(a, np.float32))
    return np.ascontiguousarray(np.concatenate(parts, 1)), col


def program(nc, d, col):
    with ExitStack() as ctx:
        R = Region(nc, ctx, "keep")
        keep = named(
            params=R.sb("params", [P, KT, NPAR]), eps=R.sb("eps", [P, 4]),
            const=lambda n: d.consts[:, col[n][0]:col[n][0] + col[n][1]], col=col)
        with ExitStack() as first:
            L = Region(nc, first, "rwkv")
            lora = [L.sb(f"lora{n}", [LORA, T]) for n in range(2)]
            rwkv_dense(nc, keep, lora, d)
            rwkv_recurrence(nc, keep, lora, d)
        out_dense(nc, keep, d, "o0", d.rwkv_wo, d.xT, "post0", "pre1")
        hgrn(nc, keep, d)
        out_dense(nc, keep, d, "o1", d.hgrn_wo, d.x1, "post1", None)


def kernel(**inputs):
    import concourse.bacc as _bacc
    from concourse.bass_utils import run_bass_kernel_spmd as _run

    nc = _bacc.Bacc("TRN2", target_bir_lowering=False, num_devices=1)
    arrays = {}

    def give(name, a):
        a = np.ascontiguousarray(a)
        arrays["in_" + name] = a
        return nc.dram_tensor("in_" + name, a.shape, mybir.dt.from_np(a.dtype), kind="ExternalInput").ap()

    def make(name, shape, kind="ExternalOutput"):
        if kind:
            return nc.dram_tensor(name, shape, F32, kind=kind).ap()
        return nc.dram_tensor(name, shape, F32).ap()

    g = {n: np.asarray(a) for n, a in inputs.items()}

    def channels(v):
        return np.asarray(v).reshape(KT, P).T

    def weight_tiles(w):
        n = w.shape[1] // P
        return w.reshape(KT, P, n, P).transpose(2, 1, 0, 3).reshape(n, P, D)

    tokens = np.concatenate([g["x_prompt"][0], g["x_sample"].reshape(SMP, D)])
    rows = {"pre0": g["norm_pre"][0], "pre1": g["norm_pre"][1], "post0": g["norm_post"][0],
            "post1": g["norm_post"][1], "w0": g["rwkv_w0"][0], "a0": g["rwkv_a0"][0],
            "k_k": g["rwkv_k_k"][0], "k_a": g["rwkv_k_a"][0], "r_k": g["rwkv_r_k"][0].reshape(D),
            "ln_w": g["rwkv_ln_w"][0], "ln_b": g["rwkv_ln_b"][0], "lb": g["hgrn_lb_logits"][0],
            "norm_w": np.concatenate([g["hgrn_norm_w"][0]] * KT)}
    for n in range(6):
        rows[f"mu{n}"] = g["rwkv_mu"][0, n]
    table, col = const_table()
    h4 = weight_tiles(g["hgrn_w_in"][0]).reshape(4, KT, P, D)
    d = named(
        xT=give("x", tokens.T.reshape(KT, P, T)),
        shiftT=give("shift", g["state_rwkv_shift"][0].T.reshape(KT, P, NB).transpose(1, 0, 2)),
        params=give("params", np.stack([channels(rows[n]) for n in PAR], 2)),
        consts=give("consts", table),
        w1=give("w1", np.stack([w.reshape(KT, P, LORA).transpose(1, 0, 2)
                                for w in (g["rwkv_w1"][0], g["rwkv_a1"][0])])),
        w2=give("w2", np.stack([w.reshape(LORA, KT, P).transpose(1, 0, 2)
                                for w in (g["rwkv_w2"][0], g["rwkv_a2"][0])])),
        w_in=give("w_in", np.concatenate([weight_tiles(g["rwkv_w_in"][0, n]) for n in range(4)])),
        rwkv_wo=give("rwkv_wo", weight_tiles(g["rwkv_w_o"][0])),
        hgrn_in=give("hgrn_in", np.stack([h4[1], h4[0], h4[3], h4[2]], 1).reshape(4 * KT, P, D)),
        hgrn_wo=give("hgrn_wo", weight_tiles(g["hgrn_w_o"][0])),
        wkv=give("wkv", g["state_rwkv_wkv"][0].transpose(1, 3, 0, 2).reshape(KT, P, NB, HD)),
        hgrn_s=give("hgrn_s", g["state_hgrn"][0].transpose(1, 2, 0, 3)),
        rkvz=[make(f"scr_{n}", (KT, P, T), None) for n in "rkvz"],
        yz=make("scr_yz", (KT, P, T), None), x1=make("scr_x1", (KT, P, T), None),
        h1=make("scr_h1", (KT, P, T), None),
        last=make("out_last", (P, KT, NB + 1)),
        wkv_p=make("out_wkv_p", (KT, P, HD)), wkv_s=make("out_wkv_s", (KT, P, NB, HD)),
        hgrn_p=make("out_hgrn_p", (KT, P, P)), hgrn_so=make("out_hgrn_s", (KT, P, NB, P)),
        y_out=make("out_y", (KT, P, T)))
    program(nc, d, col)
    r = _run(nc, [arrays], core_ids=[0]).results[0]
    y = r["out_y"].reshape(D, T).T
    last = r["out_last"].transpose(2, 1, 0).reshape(NB + 1, D)
    heads = D // HD
    wkv_p = r["out_wkv_p"].reshape(heads, HD, HD).transpose(0, 2, 1)
    wkv_s = r["out_wkv_s"].reshape(heads, HD, NB, HD).transpose(2, 0, 3, 1)
    c = np.ascontiguousarray
    return (c(y[:SEQ][None]), c(y[SEQ:].reshape(NB, DS, D)), c(last[:1][None]), c(wkv_p[None, None]),
            c(r["out_hgrn_p"][None, None]), c(last[1:][None]), c(wkv_s[None]),
            c(r["out_hgrn_s"].transpose(2, 0, 1, 3)[None]))
```
